# Optimizing a Trainium2 kernel written in Bass

```python
import jax
import jax.numpy as jnp
from jax import lax
import numpy as np

D_MODEL = 1024
BATCH = 1
SEQ = 512
DEPTH = 2

HEAD_DIM = 64
N_HEADS_A = D_MODEL // HEAD_DIM // 2
N_GROUPS_B = D_MODEL // HEAD_DIM // 2
WIDTH_A = N_HEADS_A * HEAD_DIM
WIDTH_B = N_GROUPS_B * HEAD_DIM
MIX_WIDTH = WIDTH_A + WIDTH_B
MIX_IN_WIDTH = 3 * WIDTH_A + 2 * WIDTH_B
DILATED_PATTERNS = ((128, 1), (512, 4), (2048, 16))
SGU_CHUNK = 128
RWKV_HEADS = D_MODEL // HEAD_DIM
D_DECAY_LORA = 64
D_AAA_LORA = 64
D_MV_LORA = 32
D_GATE_LORA = 160
RWKV_GN_EPS = 64e-5
N_EXPERTS = 16
N_EXPERT_GROUPS = 4
EXPERTS_PER_GROUP = N_EXPERTS // N_EXPERT_GROUPS
TOP_K = 2
D_EXPERT = 256
N_EVEN = (DEPTH + 1) // 2
N_ODD = DEPTH // 2
RMS_EPS = 1e-6

kernel_name = 'hybrid_dilated_sgu_rwkv7_grouped_moe'

def _rmsnorm(x):
    xf = x.astype(jnp.float32)
    return (xf * lax.rsqrt(jnp.mean(xf * xf, axis=-1, keepdims=True) + RMS_EPS)).astype(x.dtype)

def _ada(c_act, w, b):
    shift, scale, gate = jnp.split(c_act @ w + b, 3, axis=-1)
    return shift[:, None], scale[:, None], gate[:, None]

def _from_sub(t, S, L):
    B, R = t.shape[0], t.shape[1]
    rest = t.shape[4:]
    t = t.reshape((B, R, -1) + rest)[:, :, :L]
    return jnp.swapaxes(t, 1, 2).reshape((B, L * R) + rest)[:, :S]

def _dilated_branch(q, k, v, dilation, span):
    B, S, H, Dh = q.shape
    L = -(-S // dilation)
    n_blk = -(-L // span)
    Lp = n_blk * span

    def to_sub(t):
        t = jnp.pad(t, ((0, 0), (0, L * dilation - S), (0, 0), (0, 0)))
        t = jnp.swapaxes(t.reshape(B, L, dilation, H, Dh), 1, 2)
        t = jnp.pad(t, ((0, 0), (0, 0), (0, Lp - L), (0, 0), (0, 0)))
        return t.reshape(B, dilation, n_blk, span, H, Dh)

    def with_prev(t):
        prev = jnp.pad(t, ((0, 0), (0, 0), (1, 0), (0, 0), (0, 0), (0, 0)))[:, :, :-1]
        return jnp.concatenate([prev, t], axis=3)

    qb = to_sub(q)
    kw = with_prev(to_sub(k))
    vw = with_prev(to_sub(v))
    s = jnp.einsum('brnqhd,brnkhd->brnhqk', qb, kw).astype(jnp.float32) * (Dh ** -0.5)
    q_pos = jnp.arange(span)[:, None] + span
    k_pos = jnp.arange(2 * span)[None, :]
    dist = q_pos - k_pos
    band = (dist >= 0) & (dist <= span)
    no_prev = (jnp.arange(n_blk)[:, None, None] == 0) & (k_pos[None] < span)
    valid = band[None] & ~no_prev
    s = jnp.where(valid[:, None], s, -jnp.inf)
    m = jnp.max(s, axis=-1, keepdims=True)
    p = jnp.exp(s - m)
    den = jnp.sum(p, axis=-1, keepdims=True)
    o = jnp.einsum('brnhqk,brnkhd->brnhqd', p, vw.astype(jnp.float32)) / den
    lse = (m + jnp.log(den))[..., 0]
    o = jnp.swapaxes(o, 3, 4)
    lse = jnp.swapaxes(lse, 3, 4)
    return _from_sub(o, S, L), _from_sub(lse, S, L)

def _dilated_attention(q, k, v):
    outs, lses = [], []
    for window, dilation in DILATED_PATTERNS:
        o, lse = _dilated_branch(q, k, v, dilation, window // dilation)
        outs.append(o)
        lses.append(lse)
    wts = jax.nn.softmax(jnp.stack(lses), axis=0)
    o = jnp.sum(wts[..., None] * jnp.stack(outs), axis=0)
    return o.astype(q.dtype)

def _spatial_gating(u, z, norm_g, w_s, b_s):
    B, S, _ = u.shape
    u = jax.nn.gelu(u, approximate=False)
    z = _rmsnorm(jax.nn.gelu(z, approximate=False)) * norm_g
    zc = z.reshape(B, S // SGU_CHUNK, SGU_CHUNK, N_GROUPS_B, HEAD_DIM)
    causal = jnp.tril(jnp.ones((SGU_CHUNK, SGU_CHUNK), dtype=bool))
    w = jnp.where(causal, w_s, 0)
    mixed = jnp.einsum('gij,bcjgd->bcigd', w, zc) + b_s.T[:, :, None]
    return u * mixed.reshape(B, S, WIDTH_B)

def _even_mixer(h, w_in, w_out, sgu_norm_g, sgu_w, sgu_b):
    B, S, _ = h.shape
    proj = h @ w_in
    q, k, v, u, z = jnp.split(proj, [WIDTH_A, 2 * WIDTH_A, 3 * WIDTH_A, 3 * WIDTH_A + WIDTH_B], axis=-1)
    heads = lambda t: t.reshape(B, S, N_HEADS_A, HEAD_DIM)
    o_a = _dilated_attention(heads(q), heads(k), heads(v)).reshape(B, S, WIDTH_A)
    o_b = _spatial_gating(u, z, sgu_norm_g, sgu_w, sgu_b)
    return jnp.concatenate([o_a, o_b], axis=-1) @ w_out

def _wkv7(r, w_log, k, v, a, b):
    B, T, H, N = r.shape
    f32 = jnp.float32
    decay = jnp.exp(-jnp.exp(w_log.astype(f32)))
    seq = tuple(jnp.moveaxis(t.astype(f32), 1, 0) for t in (r, decay, k, v, a, b))

    def step(state, inp):
        r_t, w_t, k_t, v_t, a_t, b_t = inp
        sa = jnp.einsum('bhvk,bhk->bhv', state, a_t)
        state = (state * w_t[:, :, None, :] + sa[..., None] * b_t[:, :, None, :]
                 + v_t[..., None] * k_t[:, :, None, :])
        return state, jnp.einsum('bhvk,bhk->bhv', state, r_t)

    _, y = lax.scan(step, jnp.zeros((B, H, N, N), f32), seq)
    return jnp.moveaxis(y, 0, 1)

def _rwkv7_time_mix(h, v_first, vres, mu, w_rkv, w_o, w0, w1, w2, a0, a1, a2,
                    g1, g2, k_k, k_a, r_k, ln_w, ln_b):
    B, T, C = h.shape
    H, N = RWKV_HEADS, HEAD_DIM
    xx = jnp.pad(h, ((0, 0), (1, 0), (0, 0)))[:, :-1] - h
    xr, xw, xk, xv, xa, xg = [h + xx * mu[i] for i in range(6)]
    r = xr @ w_rkv[0]
    k = xk @ w_rkv[1]
    v = xv @ w_rkv[2]
    w = -jax.nn.softplus(-(w0 + jnp.tanh(xw @ w1) @ w2)) - 0.5
    if vres is None:
        v_first = v
    else:
        v0, v1, v2 = vres
        v = v + (v_first - v) * jax.nn.sigmoid(v0 + (xv @ v1) @ v2)
    a = jax.nn.sigmoid(a0 + (xa @ a1) @ a2)
    g = jax.nn.sigmoid(xg @ g1) @ g2
    heads = lambda t: t.reshape(B, T, H, N)
    kk = heads(k * k_k).astype(jnp.float32)
    kk = kk / jnp.maximum(jnp.linalg.norm(kk, axis=-1, keepdims=True), 1e-12)
    k = k * (1 + (a - 1) * k_a)
    rh, kh, vh, ah = heads(r), heads(k), heads(v), heads(a).astype(jnp.float32)
    y = _wkv7(rh, heads(w), kh, vh, -kk, kk * ah)
    mean = jnp.mean(y, axis=-1, keepdims=True)
    var = jnp.mean(jnp.square(y - mean), axis=-1, keepdims=True)
    y = ((y - mean) * lax.rsqrt(var + RWKV_GN_EPS)).reshape(B, T, C).astype(h.dtype)
    y = y * ln_w + ln_b
    y = y + (jnp.sum(rh * kh * r_k, axis=-1, keepdims=True) * vh).reshape(B, T, C)
    return (y * g) @ w_o, v_first

def _moe(h, router_w, router_b, w1, w3, w2):
    B, S, D = h.shape
    t = h.reshape(-1, D)
    n_tok = t.shape[0]
    s = jax.nn.sigmoid(t.astype(jnp.float32) @ router_w.astype(jnp.float32))
    sel = (s + router_b.astype(jnp.float32)).reshape(n_tok, N_EXPERT_GROUPS, EXPERTS_PER_GROUP)
    group_score = jnp.sum(lax.top_k(sel, TOP_K)[0], axis=-1)
    g_idx = jnp.argmax(group_score, axis=-1)
    in_group = sel[jnp.arange(n_tok), g_idx]
    _, local = lax.top_k(in_group, TOP_K)
    e_idx = g_idx[:, None] * EXPERTS_PER_GROUP + local
    wts = jnp.take_along_axis(s, e_idx, axis=1)
    wts = wts / jnp.sum(wts, axis=-1, keepdims=True)
    gates = jnp.sum(jax.nn.one_hot(e_idx, N_EXPERTS, dtype=jnp.float32) * wts[..., None], axis=1)
    gates = gates.astype(t.dtype)
    y = jnp.zeros_like(t)
    for e in range(N_EXPERTS):
        hid = jax.nn.silu(t @ w1[e]) * (t @ w3[e])
        y = y + gates[:, e:e + 1] * (hid @ w2[e])
    return y.reshape(B, S, D)

def setup_inputs(seed: int = 0) -> dict:
    key = jax.random.key(seed)
    ks = iter(jax.random.split(key, 48))
    nrm = lambda shape, scale: jax.random.normal(next(ks), shape, jnp.float32) * scale
    D = D_MODEL
    inp = {}
    inp['x'] = nrm((BATCH, SEQ, D), 1.0)
    inp['c'] = nrm((BATCH, D), 1.0)
    inp['ada_w'] = nrm((DEPTH, 2, D, 3 * D), 0.5 * D ** -0.5)
    inp['ada_b'] = nrm((DEPTH, 2, 3 * D), 0.02)
    inp['mix_w_in'] = nrm((N_EVEN, D, MIX_IN_WIDTH), D ** -0.5)
    inp['mix_w_out'] = nrm((N_EVEN, MIX_WIDTH, D), MIX_WIDTH ** -0.5)
    inp['sgu_norm_g'] = 1.0 + nrm((N_EVEN, WIDTH_B), 0.05)
    inp['sgu_w'] = nrm((N_EVEN, N_GROUPS_B, SGU_CHUNK, SGU_CHUNK), SGU_CHUNK ** -0.5)
    inp['sgu_b'] = 1.0 + nrm((N_EVEN, N_GROUPS_B, SGU_CHUNK), 0.1)
    inp['rwkv_mu'] = jax.random.uniform(next(ks), (N_ODD, 6, D), jnp.float32)
    inp['rwkv_w_rkv'] = nrm((N_ODD, 3, D, D), D ** -0.5)
    inp['rwkv_w_o'] = nrm((N_ODD, D, D), D ** -0.5)
    inp['rwkv_w0'] = jax.random.uniform(next(ks), (N_ODD, D), jnp.float32, -6.5, -1.5)
    inp['rwkv_w1'] = nrm((N_ODD, D, D_DECAY_LORA), D ** -0.5)
    inp['rwkv_w2'] = nrm((N_ODD, D_DECAY_LORA, D), 0.1 * D_DECAY_LORA ** -0.5)
    inp['rwkv_a0'] = nrm((N_ODD, D), 0.1)
    inp['rwkv_a1'] = nrm((N_ODD, D, D_AAA_LORA), D ** -0.5)
    inp['rwkv_a2'] = nrm((N_ODD, D_AAA_LORA, D), D_AAA_LORA ** -0.5)
    inp['rwkv_v0'] = 1.0 + nrm((N_ODD - 1, D), 0.1)
    inp['rwkv_v1'] = nrm((N_ODD - 1, D, D_MV_LORA), D ** -0.5)
    inp['rwkv_v2'] = nrm((N_ODD - 1, D_MV_LORA, D), D_MV_LORA ** -0.5)
    inp['rwkv_g1'] = nrm((N_ODD, D, D_GATE_LORA), D ** -0.5)
    inp['rwkv_g2'] = nrm((N_ODD, D_GATE_LORA, D), D_GATE_LORA ** -0.5)
    inp['rwkv_k_k'] = 0.85 + nrm((N_ODD, D), 0.05)
    inp['rwkv_k_a'] = 1.0 + nrm((N_ODD, D), 0.05)
    inp['rwkv_r_k'] = nrm((N_ODD, RWKV_HEADS, HEAD_DIM), 0.1)
    inp['rwkv_ln_w'] = 1.0 + nrm((N_ODD, D), 0.05)
    inp['rwkv_ln_b'] = nrm((N_ODD, D), 0.02)
    inp['router_w'] = nrm((D, N_EXPERTS), D ** -0.5)
    inp['router_b'] = nrm((N_EXPERTS,), 0.01)
    inp['moe_w1'] = nrm((DEPTH, N_EXPERTS, D, D_EXPERT), D ** -0.5)
    inp['moe_w3'] = nrm((DEPTH, N_EXPERTS, D, D_EXPERT), D ** -0.5)
    inp['moe_w2'] = nrm((DEPTH, N_EXPERTS, D_EXPERT, D), D_EXPERT ** -0.5)
    inp['final_norm_g'] = 1.0 + nrm((D,), 0.05)
    return inp

def reference(x, c, ada_w, ada_b, mix_w_in, mix_w_out, sgu_norm_g, sgu_w, sgu_b,
              rwkv_mu, rwkv_w_rkv, rwkv_w_o, rwkv_w0, rwkv_w1, rwkv_w2,
              rwkv_a0, rwkv_a1, rwkv_a2, rwkv_v0, rwkv_v1, rwkv_v2,
              rwkv_g1, rwkv_g2, rwkv_k_k, rwkv_k_a, rwkv_r_k, rwkv_ln_w, rwkv_ln_b,
              router_w, router_b, moe_w1, moe_w3, moe_w2, final_norm_g):
    c_act = jax.nn.silu(c)
    v_first = None
    for layer in range(DEPTH):
        i = layer // 2
        shift, scale, gate = _ada(c_act, ada_w[layer, 0], ada_b[layer, 0])
        h = _rmsnorm(x) * (1 + scale) + shift
        if layer % 2 == 0:
            y = _even_mixer(h, mix_w_in[i], mix_w_out[i], sgu_norm_g[i], sgu_w[i], sgu_b[i])
        else:
            vres = None if i == 0 else (rwkv_v0[i - 1], rwkv_v1[i - 1], rwkv_v2[i - 1])
            y, v_first = _rwkv7_time_mix(
                h, v_first, vres, rwkv_mu[i], rwkv_w_rkv[i], rwkv_w_o[i],
                rwkv_w0[i], rwkv_w1[i], rwkv_w2[i], rwkv_a0[i], rwkv_a1[i], rwkv_a2[i],
                rwkv_g1[i], rwkv_g2[i], rwkv_k_k[i], rwkv_k_a[i], rwkv_r_k[i],
                rwkv_ln_w[i], rwkv_ln_b[i])
        x = x + gate * y
        shift, scale, gate = _ada(c_act, ada_w[layer, 1], ada_b[layer, 1])
        h = _rmsnorm(x) * (1 + scale) + shift
        x = x + gate * _moe(h, router_w, router_b, moe_w1[layer], moe_w3[layer], moe_w2[layer])
    return _rmsnorm(x) * final_norm_g


_drawn_inputs = setup_inputs


def setup_inputs(seed=0):
    import zlib

    import numpy as np

    out = dict(_drawn_inputs(seed))
    spreads = {}
    factors = {'sgu_norm_g': 3.037,
     'rwkv_w1': 8.0,
     'rwkv_w2': 8.0,
     'rwkv_a0': 5.474,
     'rwkv_ln_w': 3.183,
     'rwkv_ln_b': 8.0}
    for name, (base, spread) in spreads.items():
        noise = np.random.default_rng([zlib.crc32(name.encode()), seed]).standard_normal(out[name].shape)
        drawn = base * np.exp(spread * noise) if base else spread * noise
        out[name] = jnp.asarray(drawn.astype(out[name].dtype))
    for name, factor in factors.items():
        out[name] = (out[name] * factor).astype(out[name].dtype)
    return out
```

```python
from contextlib import ExitStack

import concourse.bass as bass
from concourse import mybir
from concourse.alu_op_type import AluOpType as ALU

F32 = mybir.dt.float32
I32 = mybir.dt.int32
ACT = mybir.ActivationFunctionType
AX = mybir.AxisListType.X

P = 128
D = 1024
S = 512
NB = S // P
KC = D // P
HD = 64
NHA = 8
WA = NHA * HD
NEXP, NGRP, EPG, DEXP = 16, 4, 4, 256
NADA = 4
SPAN = 128
EPS = 1e-6
GN_EPS = 64e-5
KAPPA = float(2.718281828459045 ** -0.5)
NEG = 1e30
MAX_ITEMS = 24
RING = 6
LONG = 2


def bank_plan():
    plan, count = [], {}

    def add(kind, ring="a"):
        plan.append((kind, count.get(kind, 0), ring))
        count[kind] = count.get(kind, 0) + 1

    def norm():
        for c in range(KC):
            add("xTa" if c % 2 else "xTv")

    add("vec")
    add("vec")
    add("mod")
    norm()
    for kind in ("q", "k", "v", "u", "z"):
        for _ in range(4):
            add(kind)
    add("mod")
    for n in range(NB * NHA + 2):
        if n < NB * NHA:
            add("score")
        if n >= 1 and n - 1 < NB * NHA:
            add("pT")
        if n >= 2:
            if (n - 2) % NHA == 0:
                add("o", "b")
        if n >= 2 and (n - 2) % NHA == NHA - 1:
            add("oT")
    add("swT")
    add("swT")
    for b in range(NB):
        add("mix")
    for b in range(NB):
        add("sT")
    add("mod")
    for layer in range(2):
        if layer == 1:
            norm()
            rwkv_plan(add)
        add("gate")
        add("gate")
        for _ in range(2 * NB):
            add("y")
        if layer == 0:
            add("mod")
        norm()
        add("logit")
        add("rank")
        add("list")
        add("gate")
        add("gate")
    return plan


def rwkv_plan(add):
    add("wl")
    add("al")
    add("gl")
    add("gl")
    for kind in ("v1", "r1", "k1"):
        for _ in range(8):
            add(kind)
    for _ in range(KC):
        add("zw")
        add("za")
        add("nrm")
    for step in scan_steps():
        kind = step[0]
        if kind == "turn":
            add("bkT")
            add("bkT")
            add("bon")
        elif kind == "scores":
            add("sc")
        elif kind == "lower":
            add("lo")
        elif kind == "X":
            add("X")
        elif kind == "T":
            if step[3] < LEVELS - 1:
                add("Tn")
            add("Tt")
        elif kind in ("R", "U", "Y", "dS"):
            add(kind)
    for _ in range(2 * NB):
        add("g")
    for _ in range(KC):
        add("yT")


LEVELS = 6


def scan_steps():
    steps = [("prep", 0)]
    for c in range(KC + 1):
        walk = []
        if c >= 1:
            for j in range(NB):
                walk += [[("R", c - 1, h, j) for h in range(2)],
                         [("U", c - 1, h, j) for h in range(2)],
                         [("Y", c - 1, h, j) for h in range(2)]
                         + [("dS", c - 1, h, j) for h in range(2) if j < NB - 1]]
        if c < KC:
            steps.append(("turn", c))
            for h in range(2):
                for j in range(NB):
                    steps.append(("scores", c, h, j))
            for h in range(2):
                steps.append(("lower", c, h))
            for lv in range(LEVELS):
                steps += [("X", c, h, lv) for h in range(2)]
                if walk:
                    steps += walk.pop(0)
                if lv == 2 and c + 1 < KC:
                    steps.append(("prep", c + 1))
                steps += [("T", c, h, lv) for h in range(2)]
                if walk:
                    steps += walk.pop(0)
        for w in walk:
            steps += w
        if c >= 1:
            steps.append(("norm", c - 1))
    return steps


FILLED_TOGETHER = {
    "xT": ("xTa", "xTv"), "mod": ("vec", "mod"), "mixer_in": ("q", "k", "v", "u", "z"),
    "attention": ("score", "pT", "oT"), "gating": ("swT", "mix", "sT"),
    "rwkv_in": ("wl", "al", "gl", "v1", "r1", "k1", "zw", "za", "nrm"),
    "triangles": ("bkT", "bon", "sc", "lo", "X", "Tn", "Tt"), "walk": ("R", "U", "Y", "dS"), "rwkv_out": ("g", "yT"),
    "route": ("logit", "rank", "list"), "y": ("y",), "gate": ("gate",), "o": ("o",)}
EMPTIED_TOGETHER = {
    "mod_dve": ("vec", "mod"), "xT_act": ("xTa",), "xT_dve": ("xTv",), "mixer_in_act": ("k", "u", "z"),
    "mixer_in_dve": ("q", "v"), "mixer_act": ("pT", "oT", "swT", "sT"), "mixer_dve": ("score", "mix"), "o_dve": ("o",),
    "rwkv_in_act": ("wl", "al", "gl", "v1", "r1", "zw", "za"), "rwkv_in_dve": ("k1", "nrm"),
    "scan_act": ("bkT", "lo", "X", "U", "Y"), "scan_dve": ("bon", "sc", "Tn", "Tt", "R", "dS"),
    "y_dve": ("g", "y"), "gate_act": ("yT", "gate", "logit"), "route_dve": ("rank", "list")}


def shared(plan, families, what, sem):
    sems, value = {}, {}
    for family, kinds in families.items():
        count = 0
        for kind, n, _ in plan:
            if kind in kinds:
                count += 1
                value[kind, n + 1] = count
                sems[kind] = sem(f"{family}_{what}")
    return sems, lambda kind, n: (sems[kind], value[kind, n])


def build(nc, io):
    ctx = ExitStack()
    with ctx:
        def sb(name, shape, dt=F32):
            return ctx.enter_context(nc.sbuf_tensor(name, shape, dt))

        sems = {}

        def sem(name):
            if name not in sems:
                sems[name] = ctx.enter_context(nc.semaphore(name))
            return sems[name]

        arena = sb("arena", [P, 8, 4096])

        def area(i, pattern=None, **kw):
            a = arena[:, i, :]
            return a.rearrange(pattern, **kw) if pattern else a

        X = area(0, "p (b f) -> p b f", b=NB)
        HT = area(1, "p (c t) -> p c t", c=KC)
        XN = area(2, "p (b f) -> p b f", b=NB)
        qT = arena[:, 3, 0:2048].rearrange("p (f t) -> p f t", f=4)
        kT = arena[:, 3, 2048:4096].rearrange("p (f t) -> p f t", f=4)
        V0 = arena[:, 4, 0:2048].rearrange("p (b f) -> p b f", b=NB)
        U0 = arena[:, 4, 2048:4096].rearrange("p (b f) -> p b f", b=NB)
        Z0 = arena[:, 5, 0:2048].rearrange("p (b f) -> p b f", b=NB)
        SW = arena[:, 5, 2048:3072].rearrange("p (g j) -> p g j", g=NHA)
        SWT = arena[:, 5, 3072:4096].rearrange("p (g j) -> p g j", g=NHA)
        Pb = arena[:, 2, 0:1536].rearrange("p (n s) -> p n s", n=3)
        PT = arena[:, 2, 1536:3072].rearrange("p (n s) -> p n s", n=3)
        OB = arena[:, 2, 3072:4096].rearrange("p (n s) -> p n s", n=2)
        acc = arena[:, 6:8, :].rearrange("p a n -> p (a n)")[:, 0:3072]
        aring = arena[:, 6:8, :].rearrange("p a n -> p (a n)")[:, 3072:7680].rearrange("p (n f) -> p n f", n=3)
        sqz = arena[:, 6:8, :].rearrange("p a n -> p (a n)")[:, 7680:8192]
        WR = sb("WR", [P, 2, KC, 512])
        W2 = sb("W2", [P, 2, 2, D])
        LO = sb("LO", [P, 2304])
        TWA2 = sb("TWA2", [P, 2 * S])
        TWA = TWA2[:, 0:S]
        TG = sb("TG", [P, 2, S])

















        ident = sb("ident", [P, P])
        ones = sb("ones", [P, P])
        blk = sb("blk", [P, P])
        upper = sb("upper", [P, P])
        w2flat = W2[:, :, :, :].rearrange("p a b c -> p (a b c)")
        MA = w2flat[:, 0:512]
        MU = w2flat[:, 512:1024]
        DI = w2flat[:, 1024:1536].bitcast(I32)
        VA = LO[:, 0:P]
        VB = LO[:, P:2 * P]
        vecA = sb("vecA", [P, 104])
        vecB = sb("vecB", [P, 104])
        cact = sb("cact", [P, KC])
        MOD = sb("MOD", [P, NADA, 24])
        GB = sb("GB", [P, D])
        DG = TG[:, :, :].rearrange("p a (b c) -> p (a b) c", c=P)
        ss = sb("ss", [P, NB])
        ms = sb("ms", [P, NB])
        rstd = sb("rstd", [P, NB])
        mhalf = sb("mhalf", [P, 8])
        mx = sb("mx", [P, 3])
        den = sb("den", [P, 2, NHA])
        rden = sb("rden", [P, 2, NHA])
        tmp = sb("tmp", [P, 2, 512])
        RWt = sb("RWt", [P, KC, NEXP])
        rb = sb("rb", [P, NEXP])
        ltm = sb("ltm", [P, 4, 4])
        tid = sb("tid", [P, NB])
        io128 = sb("io128", [P, P])
        W12 = sb("W12", [P, 2, NB])
        SLI = sb("SLI", [P, 2, NB], I32)
        CN = sb("CN", [1, 32], I32)
        LI = sb("LI", [P, 32], I32)
        IDX = sb("IDX", [P, 1], I32)
        bsT = vecB[:, 96:104]
        gz = sqz

        Xg = arena[:, 3, 0:1024]
        XgT = arena[:, 3, 1024:2048].rearrange("p (c t) -> p c t", c=KC)
        Yt = arena[:, 3, 2048:3072]
        sil = arena[:, 3, 3072:3328]
        hid = arena[:, 3, 3328:3584]
        hidT = arena[:, 3, 3584:3840].rearrange("p (c t) -> p c t", c=2)
        CB = arena[:, 6:8, :].rearrange("p a n -> p (a n)").rearrange("p (k f) -> p k f", k=8)

        xn_dram = nc.dram_tensor("xn_rows", (S, D), F32, kind="Internal").ap()
        y_dram = nc.dram_tensor("expert_rows", (MAX_ITEMS * P, D), F32, kind="Internal").ap()

        PS = ctx.enter_context(nc.psum_tensor("PS", [P, 8, 512], F32))

        SG = LO[:, 0:64]
        CH = LO[:, 832:896].rearrange("p (b e) -> p b e", b=NB)
        HOTI = LO[:, 896:1096].rearrange("p (k i) -> p k i", k=8)
        HOTR = LO[:, 1280:2304].rearrange("p (k r) -> p k r", k=8)
        SLF = sb("SLF", [P, 8])
        RI = sb("RI", [P, 2, 8], I32)
        RF = sb("RF", [P, 2, 8])

        def masks(v, link):
            ts, stt = nc.vector.tensor_scalar, nc.vector.scalar_tensor_tensor
            low = tmp[:, 0, :].bitcast(I32)
            v.wait_ge(sem("dist"), 1)
            link(ts(low, DI[:, :], 3, None, ALU.bitwise_and))
            link(ts(MU[:, :], low, 0.0, None, ALU.is_equal))
            link(ts(low, DI[:, :], 15, None, ALU.bitwise_and))
            link(stt(MU[:, :], low, 0.0, MU[:, :], ALU.is_equal, ALU.add))
            link(stt(MU[:, :], DI[:, :], float(SPAN), MU[:, :], ALU.is_le, ALU.add))
            link(stt(MU[:, :], DI[:, :], 0.0, MU[:, :], ALU.is_ge, ALU.mult))
            link(ts(MA[:, :], MU[:, :], 0.0, NEG, ALU.is_equal, ALU.mult))

        def route(v, link, layer, M):
            tt, ts, stt, red = (nc.vector.tensor_tensor, nc.vector.tensor_scalar, nc.vector.scalar_tensor_tensor,
                                nc.vector.tensor_reduce)
            G = NB * NGRP
            sel = LO[:, 64:128]
            A, B = LO[:, 128:384], LO[:, 384:640]
            rank, m1, m2 = LO[:, 640:704], LO[:, 704:768], LO[:, 768:832]
            at = [1096]

            def small(n):
                at[0] += n
                return LO[:, at[0] - n:at[0]]

            v1, v2, gs, grank, gsel = (small(G) for _ in range(5))
            s1, s2, su = (small(NB) for _ in range(3))
            nb, end, base = (small(NEXP) for _ in range(3))
            e3 = lambda a: a.rearrange("p (g j) -> p g j", j=EPG)
            b3 = lambda a: a.rearrange("p (b e) -> p b e", b=NB)

            def ranks(out, src, n):
                a4 = A[:, 0:16 * n].rearrange("p (g j i) -> p g j i", j=4, i=4)
                b4 = B[:, 0:16 * n].rearrange("p (g j i) -> p g j i", j=4, i=4)
                other = e3(src).unsqueeze(2).to_broadcast([P, n, 4, 4])
                own = e3(src).unsqueeze(3).to_broadcast([P, n, 4, 4])
                link(tt(a4, other, own, ALU.is_gt))
                link(tt(b4, other, own, ALU.is_equal))
                low = ltm[:, :, :].rearrange("p j i -> p (j i)").unsqueeze(1).to_broadcast([P, n, 16])
                link(tt(B[:, 0:16 * n].rearrange("p (g k) -> p g k", k=16),
                        B[:, 0:16 * n].rearrange("p (g k) -> p g k", k=16), low, ALU.mult))
                link(tt(A[:, 0:16 * n], A[:, 0:16 * n], B[:, 0:16 * n], ALU.add))
                link(red(out, A[:, 0:16 * n].rearrange("p (m i) -> p m i", i=4), AX, ALU.add))

            v.wait_ge(*free("logit", layer + 1))
            v.wait_ge(sem("rb_in"), 16)
            v.wait_ge(sem("moe_consts"), 4)
            link(tt(b3(sel), b3(SG), rb[:, :].unsqueeze(1).to_broadcast([P, NB, NEXP]), ALU.add))
            ranks(rank, sel, G)
            ts(m1, rank, 0.0, None, ALU.is_equal)
            link(ts(m2, rank, 1.0, None, ALU.is_equal))
            tt(A[:, 0:64], sel, m1, ALU.mult)
            link(tt(B[:, 0:64], sel, m2, ALU.mult))
            red(v1, e3(A[:, 0:64]), AX, ALU.add)
            link(red(v2, e3(B[:, 0:64]), AX, ALU.add))
            link(tt(gs, v1, v2, ALU.add))
            ranks(grank, gs, NB)
            link(ts(gsel, grank, 0.0, None, ALU.is_equal))
            gb = gsel.unsqueeze(2).to_broadcast([P, G, EPG])
            tt(e3(m1), e3(m1), gb, ALU.mult)
            link(tt(e3(m2), e3(m2), gb, ALU.mult))
            link(tt(CH.rearrange("p b e -> p (b e)"), m1, m2, ALU.add))
            tt(A[:, 0:64], SG, m1, ALU.mult).then_inc(M("chosen"), 1)
            link(tt(B[:, 0:64], SG, m2, ALU.mult))
            red(s1, b3(A[:, 0:64]), AX, ALU.add)
            link(red(s2, b3(B[:, 0:64]), AX, ALU.add))
            link(tt(su, s1, s2, ALU.add))
            link(nc.vector.reciprocal(su, su))
            tt(W12[:, 0, :], s1, su, ALU.mult)
            link(tt(W12[:, 1, :], s2, su, ALU.mult))
            v.wait_ge(*full("rank", layer + 1))
            ps = bank("rank", layer)
            tot = ps[:, 64:64 + NEXP]
            link(ts(nb, tot, 0.0, None, ALU.is_gt))
            for k in range(1, NB):
                link(stt(nb, tot, float(k * P), nb, ALU.is_gt, ALU.add))
            link(nc.vector.tensor_tensor_scan(end, ones[:, 0:NEXP], nb, 0.0, ALU.mult, ALU.add))
            link(tt(base, end, nb, ALU.subtract))
            link(ts(base, base, float(P), None, ALU.mult))
            tt(b3(rank), b3(ps[:, 0:64]), base.unsqueeze(1).to_broadcast([P, NB, NEXP]), ALU.add
               ).then_inc(drained["rank"], 1)
            v.wait_ge(*free("rank", layer + 1))
            tt(A[:, 0:64], rank, m1, ALU.mult)
            link(tt(B[:, 0:64], rank, m2, ALU.mult))
            red(SLF[:, 0:4], b3(A[:, 0:64]), AX, ALU.add)
            link(red(SLF[:, 4:8], b3(B[:, 0:64]), AX, ALU.add))
            sl = SLI[:, :, :].rearrange("p j b -> p (j b)")
            link(nc.vector.tensor_copy(sl, SLF[:, :]))
            ts(RI[:, 0, :], sl, P - 1, None, ALU.bitwise_and)
            link(ts(RI[:, 1, :], sl, 7, None, ALU.logical_shift_right))
            link(nc.vector.tensor_copy(RF[:, :, :], RI[:, :, :]))
            for k in range(8):
                ts(HOTR[:, k, :], io128[:, :], RF[:, 0, k:k + 1], None, ALU.is_equal)
                last = ts(HOTI[:, k, :], io128[:, 0:25], RF[:, 1, k:k + 1], tid[:, k % NB:k % NB + 1], ALU.is_equal,
                          ALU.mult)
            last.then_inc(M("hot"), 1)
            it = LO[0:1, 128:512].rearrange("p (i e) -> p i e", e=NEXP)
            link(tt(it, end[0:1].unsqueeze(1).to_broadcast([1, MAX_ITEMS, NEXP]),
                    io128[0:1, 0:MAX_ITEMS].unsqueeze(2).to_broadcast([1, MAX_ITEMS, NEXP]), ALU.is_le))
            link(red(LO[0:1, 640:664], it, AX, ALU.add))
            nc.vector.tensor_copy(CN[0:1, 1:1 + MAX_ITEMS], LO[0:1, 640:664])
            nc.vector.tensor_copy(CN[0:1, 0:1], end[0:1, NEXP - 1:NEXP])
            v.wait_ge(*full("list", layer + 1))
            nc.vector.tensor_copy(LI[:, 0:25], bank("list", layer)[:, 0:25]).then_inc(drained["list"], 1)
            v.wait_ge(*free("list", layer + 1))
            nc.vector.engine_nop().then_inc(M("items"), 1)

        XX = area(2, "p (c t) -> p c t", c=KC)
        XM = [area(3, "p (c t) -> p c t", c=KC), area(4, "p (c t) -> p c t", c=KC)]
        V1 = area(5, "p (b f) -> p b f", b=NB)
        R1 = area(6, "p (c t) -> p c t", c=KC)
        K1 = area(7, "p (c t) -> p c t", c=KC)
        SGW, AA, KK = XM[0], XM[1], XX
        RN = HT
        W1L = LO[:, 0:512].rearrange("p (c f) -> p c f", c=KC)
        A1L = LO[:, 512:1024].rearrange("p (c f) -> p c f", c=KC)
        G1L = LO[:, 1024:2304].rearrange("p (c f) -> p c f", c=KC)
        WA2 = w2flat[:, 0:1024]
        G2A = w2flat[:, 1024:2048]
        G2B = w2flat[0:32, 2048:3072]
        LNW = w2flat[:, 0:1024]
        LNB = TWA2[:, :]
        MK = w2flat[:, 3072:3584].bitcast(I32)
        t1 = arena[:, 1, :].rearrange("p (n j t) -> p n j t", n=8, j=NB)
        Tn = [t1[:, h] for h in range(2)]
        XT = [t1[:, 2 + h] for h in range(2)]
        Tt = [[t1[:, 4 + 2 * par + h] for h in range(2)] for par in range(2)]
        LT = [GB[:, h * 512:h * 512 + 512].rearrange("p (j t) -> p j t", j=NB) for h in range(2)]
        LM = [LO[:, h * 512:h * 512 + 512].rearrange("p (j t) -> p j t", j=NB) for h in range(2)]
        CU = LO[:, 1024:1536]
        E1 = LO[:, 1536:2048]
        wrf = WR[:, :, :, :].rearrange("p a b c -> p (a b c)")
        PM = [[wrf[:, (2 * par + h) * 1536:(2 * par + h + 1) * 1536].rearrange("p (j m t) -> p j m t", j=NB, m=3)
               for h in range(2)] for par in range(2)]
        BK = [wrf[:, 6144 + par * 1024:6144 + (par + 1) * 1024].rearrange("p (j m f) -> p j m f", j=NB, m=2)
              for par in range(2)]
        LV = sb("LV", [P, P])
        pairs = tmp[:, 1, 256:384]
        joins = tmp[:, 1, 384:512]
        NM = w2flat[:, 3584:4096]
        MID = sb("MID", [P, NB])
        EM = sb("EM", [P, NB])
        EE = sb("EE", [P, NB])
        DD = sb("DD", [P, 3, NB])
        BON = tmp[:, 1, 192:256].rearrange("p (c n) -> p c n", c=KC)
        RH = LO[:, 2048:2176].rearrange("p (h d) -> p h d", h=2)
        UU = LO[:, 2176:2304].rearrange("p (h d) -> p h d", h=2)
        ST = tmp[:, 1, 0:128].rearrange("p (h d) -> p h d", h=2)
        SD = tmp[:, 1, 128:192]
        oka = sb("oka", [P, KC])
        sm = sb("sm", [P, 4, 8])

        plan = bank_plan()
        drained_at = {}
        places = {"a": list(range(RING)), "b": list(range(RING, RING + LONG))}
        taken, seen = {}, {"a": 0, "b": 0}
        for kind, n, ring in plan:
            b = places[ring][seen[ring] % len(places[ring])]
            seen[ring] += 1
            drained_at[kind, n] = (b, taken.get(b))
            taken[b] = (kind, n)
        filled, full = shared(plan, FILLED_TOGETHER, "filled", sem)
        drained, free = shared(plan, EMPTIED_TOGETHER, "drained", sem)

        def bank(kind, n):
            return PS[:, drained_at[kind, n][0], :]

        def open_bank(pe, kind, n):
            b, before = drained_at[kind, n]
            if before:
                pe.wait_ge(*free(before[0], before[1] + 1))
            return PS[:, b, :]

        block = ctx.enter_context(nc.Block())

        tiles = [(io["mix_w_in"][0], n * 512) for n in range(5)] + [(io["mix_w_out"][0], n * 512) for n in range(2)]
        tile_last = [("q", 3), ("k", 3), ("v", 3), ("u", 3), ("z", 3), ("y", 3), ("y", 7)]
        for n, kind in ((2, "v1"), (0, "r1"), (1, "k1")):
            for half in range(2):
                tiles.append((io["rwkv_w_rkv"][0, n], half * 512))
                tile_last.append((kind, 4 * half + 3))
        for half in range(2):
            tiles.append((io["rwkv_w_o"][0], half * 512))
            tile_last.append(("y", 8 + 4 * half + 3))

        def tile_ready(eng, n):
            eng.wait_ge(sem(f"tile_in{n % 2}"), 16 * (n // 2 + 1))

        def moe_sem(layer, name):
            return sem(f"m{layer}_{name}")

        @block.sync
        def _(sp):
            sp.dma_start(VA[96:104, :], io["c"].rearrange("a (r p) -> (a r) p", p=P)).then_inc(sem("vec_in"), 16)
            sp.dma_start(VA[0:96, :], io["ada_b"].rearrange("l m (r p) -> (l m r) p", p=P)).then_inc(sem("vec_in"), 16)
            for r, name in ((0, "rwkv_mu"), (48, "rwkv_w0"), (56, "rwkv_a0"), (64, "rwkv_k_k"), (72, "rwkv_k_a"),
                            (80, "rwkv_r_k"), (96, "sgu_b")):
                v = io[name]
                if name == "rwkv_mu":
                    v = v.rearrange("l m (r p) -> (l m r) p", p=P)
                elif name == "rwkv_r_k":
                    v = v.rearrange("l (r two) d -> (l r) (two d)", two=2)
                elif name == "sgu_b":
                    v = v[0]
                else:
                    v = v.rearrange("l (r p) -> (l r) p", p=P)
                sp.dma_start(VB[r:r + v.shape[0], :], v).then_inc(sem("vec_in"), 16)
            sp.dma_start(VB[88:96, :], io["rwkv_w0"].rearrange("l (r p) -> (l r) p", p=P)).then_inc(sem("vec_in"), 16)
            sp.dma_start(X, io["x"][0].rearrange("(b p) f -> p b f", p=P)).then_inc(sem("x_in"), 16)

            def ada(L, m):
                n = L * 2 * KC + m
                if n >= 3:
                    sp.wait_ge(sem("ada_step"), n - 2)
                sp.dma_start(aring[:, n % 3, :],
                             io["ada_w"][L // 2, L % 2, (m % KC) * P:(m % KC + 1) * P,
                                         (m // KC) * 1536:(m // KC + 1) * 1536]
                             ).then_inc(sem(f"ada_in{n % 3}"), 16)

            def tile(n):
                if n >= 2:
                    k, at = tile_last[n - 2]
                    sp.wait_ge(*full(k, at + 1))
                w, col = tiles[n]
                sp.dma_start(WR[:, n % 2, :, :], w[:, col:col + 512].rearrange("(c p) f -> p c f", p=P)
                             ).then_inc(sem(f"tile_in{n % 2}"), 16)

            for m in range(2 * KC):
                ada(0, m)
            tile(0)
            tile(1)
            sp.dma_start(SW, io["sgu_w"][0].rearrange("g i j -> i g j")).then_inc(sem("sw_in"), 16)
            sp.dma_start(gz, io["sgu_norm_g"][0].partition_broadcast(P)).then_inc(sem("gz_in"), 16)
            sp.dma_start(RWt[:, :, :], io["router_w"].rearrange("(c p) e -> p c e", p=P)).then_inc(sem("rw_in"), 16)
            sp.dma_start(rb[:, :], io["router_b"].partition_broadcast(P)).then_inc(sem("rb_in"), 16)
            for m in range(2 * KC):
                ada(1, m)
                if m % 4 == 3 and m < 12:
                    tile(2 + m // 4)
            tile(5)
            tile(6)
            for L in (2, 3):
                for m in range(2 * KC):
                    ada(L, m)

            def moe(layer):
                M = lambda name: moe_sem(layer, name)
                sp.wait_ge(sem("xn"), NB * (2 * layer + 2))
                sp.dma_start(xn_dram.rearrange("(b p) f -> p b f", p=P), XN).then_inc(M("rows_out"), 16)
                sp.wait_ge(*full("y", 8 * (layer + 1)))
                sp.wait_ge(M("items"), 1)
                n = sp.value_load(CN[0:1, 0:1], min_val=8, max_val=MAX_ITEMS)

                def load(i, e, slot):
                    w = lambda name: io[name][layer][bass.ds(e, 1)]
                    sp.dma_start(WR[:, slot, :, 0:DEXP], w("moe_w1").rearrange("e (c p) f -> p (e c) f", p=P)
                                 ).then_inc(M("w1_in"), 16)
                    sp.dma_start(WR[:, slot, :, DEXP:2 * DEXP], w("moe_w3").rearrange("e (c p) f -> p (e c) f", p=P)
                                 ).then_inc(M("w3_in"), 16)
                    sp.dma_start(W2[:, slot, :, :], w("moe_w2").rearrange("e (c p) f -> p (e c) f", p=P)
                                 ).then_inc(M("w2_in"), 16)

                def earlier(count):
                    sp.wait_ge(M("w1_in"), count)
                    sp.wait_ge(M("w3_in"), count)
                    sp.wait_ge(M("w2_in"), count)

                for i in range(2):
                    e = sp.value_load(CN[0:1, i + 1:i + 2], min_val=0, max_val=NEXP - 1)
                    if i:
                        earlier(i * 16)
                    load(i, e, i)
                used, loaded = sp.alloc_register(f"used{layer}"), sp.alloc_register(f"loaded{layer}")
                sp.reg_mov(used, 1)
                sp.reg_mov(loaded, 32)
                with sp.Fori(2, n) as i:
                    e = sp.value_load(CN[0:1, bass.ds(i + 1, 1)], min_val=0, max_val=NEXP - 1)
                    sp.wait_ge(M("items"), 1)
                    sp.wait_ge(M("up"), used)
                    sp.wait_ge(M("down"), used)
                    earlier(loaded)
                    w = lambda name: io[name][layer][bass.ds(e, 1)]
                    slot = bass.ds(i % 2, 1)
                    sp.dma_start(WR[:, slot, :, 0:DEXP].rearrange("p s c f -> p (s c) f"),
                                 w("moe_w1").rearrange("e (c p) f -> p (e c) f", p=P)).then_inc(M("w1_in"), 16)
                    sp.dma_start(WR[:, slot, :, DEXP:2 * DEXP].rearrange("p s c f -> p (s c) f"),
                                 w("moe_w3").rearrange("e (c p) f -> p (e c) f", p=P)).then_inc(M("w3_in"), 16)
                    sp.dma_start(W2[:, slot, :, :].rearrange("p s c f -> p (s c) f"),
                                 w("moe_w2").rearrange("e (c p) f -> p (e c) f", p=P)).then_inc(M("w2_in"), 16)
                    sp.reg_add(used, used, 1)
                    sp.reg_add(loaded, loaded, 16)

            moe(0)
            n = sp.value_load(CN[0:1, 0:1], min_val=8, max_val=MAX_ITEMS)
            sp.wait_ge(sem("x_done"), 16)
            sp.wait_ge(moe_sem(0, "down"), n)
            for k in range(3):
                sp.wait_ge(moe_sem(0, f"w{k + 1}_in"), n * 16)
            sp.dma_start(W1L, io["rwkv_w1"][0].rearrange("(c p) f -> p c f", p=P)).then_inc(sem("lora_in"), 16)
            sp.dma_start(A1L, io["rwkv_a1"][0].rearrange("(c p) f -> p c f", p=P)).then_inc(sem("lora_in"), 16)
            sp.dma_start(G1L, io["rwkv_g1"][0].rearrange("(c p) f -> p c f", p=P)).then_inc(sem("lora_in"), 16)
            tile(7)
            tile(8)
            sp.dma_start(WA2[0:HD, :], io["rwkv_w2"][0]).then_inc(sem("wa2_in"), 16)
            sp.dma_start(WA2[HD:P, :], io["rwkv_a2"][0]).then_inc(sem("wa2_in"), 16)
            sp.dma_start(G2A, io["rwkv_g2"][0, 0:P, :]).then_inc(sem("g2_in"), 16)
            sp.dma_start(G2B, io["rwkv_g2"][0, P:P + 32, :]).then_inc(sem("g2_in"), 16)
            for n in range(9, 13):
                tile(n)
            sp.wait_ge(*full("za", KC))
            sp.dma_start(LNW, io["rwkv_ln_w"][0].partition_broadcast(P)).then_inc(sem("ln_in"), 16)
            sp.dma_start(LNB, io["rwkv_ln_b"][0].partition_broadcast(P)).then_inc(sem("ln_in"), 16)
            sp.wait_ge(*full("Y", 8 * KC))
            tile(13)
            tile(14)
            moe(1)
            sp.wait_ge(sem("x_done"), 32)
            sp.dma_start(LNW, io["final_norm_g"].partition_broadcast(P)).then_inc(sem("fin_in"), 16)
            for b in range(NB):
                sp.wait_ge(sem("fin"), b + 1)
                sp.dma_start(io["out"][0, b * P:(b + 1) * P, :], XN[:, b, :]).then_inc(sem("out_done"), 16)
            sp.wait_ge(sem("out_done"), 16 * NB)

        @block.gpsimd
        def _(gp):
            done = [0]

            def link(ins):
                done[0] += 1
                ins.then_inc(sem("pool_chain"), 1)
                gp.wait_ge(sem("pool_chain"), done[0])

            link(gp.memset(ident[:, :], 0.0))
            gp.affine_select(out=ident[:, :], in_=ident[:, :], compare_op=ALU.not_equal, fill=1.0, base=0,
                             pattern=[[-1, P]], channel_multiplier=1).then_inc(sem("ident_ready"), 1)
            gp.memset(ones[:, :], 1.0).then_inc(sem("ones_ready"), 1)
            gp.memset(mhalf[:, :], -0.5).then_inc(sem("mhalf_ready"), 1)
            gp.iota(DI[:, :], pattern=[[-1, S]], base=S - P, channel_multiplier=1).then_inc(sem("dist"), 1)
            gp.iota(io128[:, :], pattern=[[1, P]], base=0, channel_multiplier=0,
                    allow_small_or_imprecise_dtypes=True).then_inc(sem("moe_consts"), 1)
            gp.iota(tid[:, :], pattern=[[P, NB]], base=0, channel_multiplier=1,
                    allow_small_or_imprecise_dtypes=True).then_inc(sem("moe_consts"), 1)
            link(gp.memset(ltm[:, :, :], 1.0))
            gp.affine_select(out=ltm[:, :, :], in_=ltm[:, :, :], compare_op=ALU.is_gt, fill=0.0, base=0,
                             pattern=[[1, 4], [-1, 4]], channel_multiplier=0).then_inc(sem("moe_consts"), 1)
            link(gp.memset(upper[:, :], 1.0))
            gp.affine_select(out=upper[:, :], in_=upper[:, :], compare_op=ALU.is_gt, fill=0.0, base=0,
                             pattern=[[1, P]], channel_multiplier=-1).then_inc(sem("moe_consts"), 1)
            link(gp.memset(DG[:, :, :], 0.0))
            for n in range(MAX_ITEMS):
                gp.dma_start(y_dram[n * P:(n + 1) * P, :], DG[:, :, :].rearrange("p a b -> p (a b)")
                             ).then_inc(sem("rows_zero"), 16)

            def level(gp, c, h, lv):
                n = 2 * LEVELS * c + 2 * lv + h
                if n >= 2:
                    gp.wait_ge(*full("X", n - 1))
                if h == 0:
                    if n:
                        gp.wait_ge(sem("lm_ready"), n)
                    link(gp.tensor_scalar(joins[:, :], LV[:, :], float(lv + 2), None, ALU.is_equal))
                gp.tensor_tensor(LM[h], LT[h], joins[:, :].unsqueeze(1).to_broadcast([P, NB, P]), ALU.mult
                                 ).then_inc(sem("lm_ready"), 1)

            def rms(n, src, dst, needs, width):
                gp.wait_ge(sem("ms_ready"), n + 1)
                gp.tensor_tensor(dst, src, mhalf[:, 0:width], ALU.pow).then_inc(sem("rstd_ready"), 1)

            gp.wait_ge(sem("mhalf_ready"), 1)
            rms(0, ms[:, :], rstd[:, :], None, NB)
            gp.wait_ge(sem("sw_in"), 16)
            gp.affine_select(out=SW, in_=SW, compare_op=ALU.is_ge, fill=0.0, base=0,
                             pattern=[[0, NHA], [-1, P]], channel_multiplier=1).then_inc(sem("swm"), 1)
            rms(1, ms[:, :], rstd[:, :], None, NB)

            def moe(layer):
                M = lambda name: moe_sem(layer, name)
                rms(2 + 2 * layer, ms[:, :], rstd[:, :], None, NB)
                gp.wait_ge(M("items"), 1)
                gp.wait_ge(M("rows_out"), 16)
                n = gp.value_load(CN[0:1, 0:1], min_val=8, max_val=MAX_ITEMS)
                src = bass.IndirectOffsetOnAxis(ap=IDX[:, 0:1], axis=0)
                gp.tensor_copy(IDX[:, :], LI[:, 0:1]).then_inc(M("idx"), 1)
                gp.wait_ge(M("idx"), 1)
                gp.indirect_dma_start(Xg, None, xn_dram, src).then_inc(M("xg_in"), 16)
                indexed, turned = gp.alloc_register(f"indexed{layer}"), gp.alloc_register(f"turned{layer}")
                gathered = gp.alloc_register(f"gathered{layer}")
                gp.reg_mov(gathered, 0)
                gp.reg_mov(indexed, 2)
                gp.reg_mov(turned, 1)
                with gp.Fori(0, n) as i:
                    gp.wait_ge(M("xg_in"), i * 16 + 16)
                    gp.tensor_copy(IDX[:, :], LI[:, bass.ds(i + 1, 1)]).then_inc(M("idx"), 1)
                    gp.wait_ge(M("rows_out"), 16)
                    gp.wait_ge(M("idx"), indexed)
                    gp.wait_ge(M("tx"), turned)
                    gp.reg_add(indexed, indexed, 1)
                    gp.reg_add(turned, turned, 1)
                    gp.reg_add(gathered, gathered, 16)
                    gp.indirect_dma_start(Xg, None, xn_dram, src).then_inc(M("xg_in"), 16)
                gp.wait_ge(M("row_out"), n * 16)
                gp.reg_add(gathered, gathered, 16)
                gp.wait_ge(M("rows_out"), 16)
                gp.wait_ge(M("xg_in"), gathered)
                for b in range(NB):
                    for j in range(2):
                        gp.indirect_dma_start(CB[:, 2 * b + j, :], None, y_dram,
                                              bass.IndirectOffsetOnAxis(ap=SLI[:, j, b:b + 1], axis=0)
                                              ).then_inc(M(f"pair_in{b}"), 16)

            moe(0)
            rms(3, ms[:, :], rstd[:, :], None, NB)
            link(gp.memset(blk[:, :], 0.0))
            link(gp.memset(blk[0:HD, 0:HD], 1.0))
            gp.memset(blk[HD:P, HD:P], 1.0).then_inc(sem("blk_ready"), 1)
            gp.wait_ge(sem("blk_ready"), 1)
            link(gp.memset(NM[:, :], 1.0))
            gp.memset(NM[:, 0:S:P], 0.0).then_inc(sem("blk_ready"), 1)
            gp.wait_ge(*full("k1", 8))
            gp.memset(wrf[:, 0:6144], 0.0).then_inc(sem("zeroed"), 1)
            gp.memset(GB[:, :], 0.0).then_inc(sem("zeroed"), 1)
            gp.wait_ge(*full("gl", 2))
            gp.wait_ge(sem("levels"), 1)
            link(gp.tensor_scalar(pairs[:, :], LV[:, :], 1.0, None, ALU.is_equal))
            for step in scan_steps():
                if step[0] == "lower":
                    _, c, h = step
                    gp.wait_ge(sem("lt_ready"), NB * (2 * c + h + 1))
                    if c >= 2:
                        gp.wait_ge(*full("U", 8 * (c - 1)))
                    pairs4 = pairs[:, :].unsqueeze(1).to_broadcast([P, NB, P])
                    idb = ident[:, :].unsqueeze(1).to_broadcast([P, NB, P])
                    link(gp.tensor_tensor(Tt[c % 2][h], LT[h], pairs4, ALU.mult))
                    gp.tensor_tensor(Tt[c % 2][h], Tt[c % 2][h], idb, ALU.add).then_inc(sem("tt0"), 1)
                    level(gp, c, h, 0)
                elif step[0] == "T" and step[3] < LEVELS - 1:
                    level(gp, step[1], step[2], step[3] + 1)
                elif step[0] == "norm":
                    c = step[1]
                    g4 = lambda a: a.rearrange("p (j h) -> p j h", j=NB)
                    gp.wait_ge(sem("gn_var"), c + 1)
                    gp.tensor_tensor(sm[:, 3, :], sm[:, 2, :], mhalf[:, 0:8], ALU.pow).then_inc(sem("gn_rstd"), 1)
                    y3 = SGW[:, c, :].rearrange("p (j f) -> p j f", j=NB)
                    if c == 0:
                        gp.wait_ge(sem("ln_in"), 32)
                    bc = lambda a: a[:, c * P:(c + 1) * P].unsqueeze(1).to_broadcast([P, NB, P])
                    gp.wait_ge(sem("gn_y"), c + 1)
                    link(gp.tensor_tensor(y3, y3, bc(LNW), ALU.mult))
                    link(gp.tensor_tensor(y3, y3, bc(LNB), ALU.add))
                    v3 = V1[:, :, c * P:(c + 1) * P]
                    gp.wait_ge(sem("gn_bv"), c + 1)
                    gp.tensor_tensor(v3, v3, y3, ALU.add).then_inc(sem("y_ready"), 1)
            moe(1)
            rms(5, ms[:, :], rstd[:, :], None, NB)

        @block.scalar
        def _(act):
            def squares(n):
                if n == 0:
                    act.wait_ge(sem("x_in"), 16)
                else:
                    act.wait_ge(sem("x_done"), 8 * n)
                for b in range(NB):
                    nc.scalar.activation(XN[:, b, :], X[:, b, :], ACT.Square, accum_out=ss[:, b:b + 1]
                                         ).then_inc(sem("ss_ready"), 1)

            def hT(n, L):
                for c in range(1, KC, 2):
                    k = 4 * n + c // 2
                    act.wait_ge(*full("xTa", k + 1))
                    if c == 1:
                        act.wait_ge(sem("mod_ready"), L + 1)
                    nc.scalar.activation(HT[:, c, :], bank("xTa", k), ACT.Identity, bias=MOD[:, L, c:c + 1],
                                         scale=MOD[:, L, 8 + c:9 + c]).then_inc(drained["xTa"], 1)

            def gate(k):
                if k:
                    act.wait_ge(sem("x_done"), 8 * k)
                for half in range(2):
                    act.wait_ge(*full("gate", 2 * k + half + 1))
                    nc.scalar.copy(GB[:, half * 512:half * 512 + 512], bank("gate", 2 * k + half)
                                   ).then_inc(drained["gate"], 1)

            act.wait_ge(*free("vec", 1))
            nc.scalar.activation(cact[:, :], vecA[:, 96:104], ACT.Silu).then_inc(sem("c_ready"), 1)
            squares(0)
            hT(0, 0)
            for f in range(4):
                act.wait_ge(*full("k", f + 1))
                nc.scalar.copy(kT[:, f, :], bank("k", f)).then_inc(drained["k"], 1)
            for b in range(NB):
                act.wait_ge(*full("u", b + 1))
                nc.scalar.activation(U0[:, b, :], bank("u", b), ACT.Gelu).then_inc(drained["u"], 1)
            for b in range(NB):
                act.wait_ge(*full("z", b + 1))
                nc.scalar.activation(Z0[:, b, :], bank("z", b), ACT.Gelu).then_inc(drained["z"], 1)
                act.wait_ge(*free("z", b + 1))
                nc.scalar.activation(OB[:, 0, :], Z0[:, b, :], ACT.Square, accum_out=ss[:, b:b + 1]
                                     ).then_inc(sem("zss_ready"), 1)
            for n in range(NB * NHA + 2):
                if n < NB * NHA:
                    i = n // NHA
                    act.wait_ge(*free("score", n + 1))
                    row = Pb[:, n % 3, 0:(i + 1) * P]
                    nc.scalar.activation(row, row, ACT.Exp, bias=mx[:, n % 3:n % 3 + 1], scale=-1.0
                                         ).then_inc(sem("probs"), 1)
                if 1 <= n <= NB * NHA:
                    m = n - 1
                    i = m // NHA
                    act.wait_ge(*full("pT", m + 1))
                    if m >= 3:
                        act.wait_ge(sem("pv"), m - 2)
                    nc.scalar.copy(PT[:, m % 3, 0:(i + 1) * P], bank("pT", m)[:, 0:(i + 1) * P]
                                   ).then_inc(drained["pT"], 1)
                if n >= 2 and (n - 2) % NHA == NHA - 1:
                    i = (n - 2) // NHA
                    act.wait_ge(*full("oT", i + 1))
                    nc.scalar.copy(HT[:, 0:4, i * P:(i + 1) * P], bank("oT", i).rearrange("p (c t) -> p c t", c=4)
                                   ).then_inc(drained["oT"], 1)
            for k in range(2):
                act.wait_ge(*full("swT", k + 1))
                nc.scalar.copy(SWT[:, 4 * k:4 * k + 4, :], bank("swT", k).rearrange("p (c t) -> p c t", c=4)
                               ).then_inc(drained["swT"], 1)
            for b in range(NB):
                act.wait_ge(*full("sT", b + 1))
                nc.scalar.copy(HT[:, 4:8, b * P:(b + 1) * P], bank("sT", b).rearrange("p (c t) -> p c t", c=4)
                               ).then_inc(drained["sT"], 1)
            gate(0)

            def moe(layer):
                M = lambda name: moe_sem(layer, name)
                L = 2 * layer + 1
                squares(L)
                hT(L, L)
                act.wait_ge(*full("logit", layer + 1))
                nc.scalar.activation(SG[:, :], bank("logit", layer)[:, 0:64], ACT.Sigmoid
                                     ).then_inc(drained["logit"], 1)
                gate(L)
                act.wait_ge(M("items"), 1)
                n = act.value_load(CN[0:1, 0:1], min_val=8, max_val=MAX_ITEMS)

                def turned(wait):
                    act.wait_ge(M("tx"), wait)
                    for c in range(4):
                        last = nc.scalar.activation(XgT[:, c, :], PS[:, 0, c * P:(c + 1) * P], ACT.Identity,
                                                    bias=MOD[:, L, c:c + 1], scale=MOD[:, L, 8 + c:9 + c])
                    last.then_inc(M("xga"), 1)

                turned(1)
                with act.Fori(0, n) as i:
                    act.wait_ge(M("up"), i + 1)
                    act.wait_ge(M("hid"), i)
                    nc.scalar.activation(sil, PS[:, 2, 0:DEXP], ACT.Silu).then_inc(M("sil"), 1)
                    turned(i + 2)
                    act.wait_ge(M("yt"), i + 1)
                    act.dma_start(y_dram[bass.ds(i * P, P), :], Yt).then_inc(M("row_out"), 16)

            moe(0)

            def copy(dst, kind, k, src, func=ACT.Copy):
                act.wait_ge(*full(kind, k + 1))
                nc.scalar.activation(dst, src, func).then_inc(drained[kind], 1)

            def rwkv():
                squares(2)
                hT(2, 2)
                act.wait_ge(*full("wl", 1))
                nc.scalar.activation(TWA[0:HD, :], bank("wl", 0)[0:HD, :], ACT.Tanh).then_inc(drained["wl"], 1)
                copy(TWA[HD:P, :], "al", 0, bank("al", 0)[HD:P, :])
                copy(TG[:, 0, :], "gl", 0, bank("gl", 0), ACT.Sigmoid)
                copy(TG[0:32, 1, :], "gl", 1, bank("gl", 1)[0:32, :], ACT.Sigmoid)
                for k in range(8):
                    half, b = k // 4, k % 4
                    copy(V1[:, b, half * 512:half * 512 + 512], "v1", k, bank("v1", k))
                for c in range(KC):
                    copy(R1[:, c, :], "r1", c, bank("r1", c))
                for c in range(KC):
                    act.wait_ge(*full("zw", c + 1))
                    nc.scalar.activation(SGW[:, c, :], bank("zw", c), ACT.Sigmoid, bias=vecB[:, 48 + c:49 + c]
                                         ).then_inc(drained["zw"], 1)
                    act.wait_ge(*full("za", c + 1))
                    nc.scalar.activation(AA[:, c, :], bank("za", c), ACT.Sigmoid, bias=vecB[:, 56 + c:57 + c]
                                         ).then_inc(drained["za"], 1)
                    act.wait_ge(sem("kkr"), c + 1)
                    if c >= 2:
                        act.wait_ge(*full("nrm", c - 1))
                    sq = (CU, E1)[c % 2]
                    nc.scalar.activation(sq, KK[:, c, :], ACT.Square).then_inc(sem("ksq"), 1)
                for c in range(KC):
                    act.wait_ge(sem("kinv"), c + 1)
                    nc.scalar.activation(RN[:, c, :], RN[:, c, :], ACT.Sqrt).then_inc(sem("knorm"), 1)
                n_sc = {k: 0 for k in ("X", "R", "U", "Y")}
                for step in scan_steps():
                    kind = step[0]
                    if kind == "prep":
                        c = step[1]
                        act.wait_ge(sem("cc"), c + 1)
                        nc.scalar.activation(E1, CU, ACT.Exp, scale=-KAPPA).then_inc(sem("e1"), 1)
                        nc.scalar.activation(EM[:, :], MID[:, :], ACT.Exp, scale=-KAPPA)
                        nc.scalar.activation(EE[:, :], CU[:, P - 1:S:P], ACT.Exp, scale=-KAPPA).then_inc(sem("ee"), 1)
                        act.wait_ge(sem("ce"), c + 1)
                        nc.scalar.activation(SGW[:, c, :], SGW[:, c, :], ACT.Exp, scale=-KAPPA).then_inc(sem("e2"), 1)
                        act.wait_ge(sem("ee"), c + 1)
                        nc.scalar.activation(CU, CU, ACT.Exp, scale=KAPPA).then_inc(sem("e3"), 1)
                    elif kind == "turn":
                        c = step[1]
                        for g in range(2):
                            if c >= 2:
                                act.wait_ge(*full("dS", 6 * (c - 1)))
                            copy(BK[c % 2][:, 2 * g:2 * g + 2, :, :], "bkT", 2 * c + g,
                                 bank("bkT", 2 * c + g).rearrange("p (j m f) -> p j m f", j=2, m=2))
                    elif kind == "lower":
                        _, c, h = step
                        copy(Tn[h], "lo", 2 * c + h, bank("lo", 2 * c + h).rearrange("p (j t) -> p j t", j=NB))
                    elif kind == "X":
                        _, c, h, lv = step
                        n = n_sc["X"]
                        n_sc["X"] += 1
                        if n >= 2:
                            act.wait_ge(*full("Tt", n - 1))
                        copy(XT[h], "X", n, bank("X", n).rearrange("p (j t) -> p j t", j=NB))
                    elif kind == "U":
                        _, c, h, j = step
                        n = n_sc["U"]
                        n_sc["U"] += 1
                        if n >= 2:
                            act.wait_ge(*full("Y", n - 1))
                        if j and n >= 2:
                            act.wait_ge(*full("dS", 6 * c + 2 * (j - 1) + h + 1))
                        copy(UU[:, h, :], "U", n, bank("U", n)[:, 0:HD])
                    elif kind == "Y":
                        _, c, h, j = step
                        n = n_sc["Y"]
                        n_sc["Y"] += 1
                        act.wait_ge(sem("prep_done"), c + 1)
                        copy(SGW[:, c, j * P + h * HD:j * P + (h + 1) * HD], "Y", n, bank("Y", n)[:, 0:HD])
                    elif kind == "norm":
                        c = step[1]
                        act.wait_ge(sem("gn_mean"), c + 1)
                        nc.scalar.activation(KK[:, c, :], SGW[:, c, :], ACT.Square).then_inc(sem("gn_sq"), 1)
                for c in range(KC):
                    copy(HT[:, c, :], "yT", c, bank("yT", c))
                gate(2)

            rwkv()
            moe(1)
            squares(4)

        @block.vector
        def _(v):
            done = [0]

            def link(ins):
                done[0] += 1
                ins.then_inc(sem("dve_chain"), 1)
                v.wait_ge(sem("dve_chain"), done[0])

            tt, ts, stt, red = (nc.vector.tensor_tensor, nc.vector.tensor_scalar, nc.vector.scalar_tensor_tensor,
                                nc.vector.tensor_reduce)

            def ada(L, m):
                n = L * 2 * KC + m
                c, half = m % KC, m // KC
                a = acc[:, half * 1536:(half + 1) * 1536]
                v.wait_ge(sem(f"ada_in{n % 3}"), 16 * (n // 3 + 1))
                if n == 0:
                    v.wait_ge(sem("c_ready"), 1)
                else:
                    v.wait_ge(sem("ada_step"), n)
                if c == 0:
                    if L:
                        v.wait_ge(*full("mod", L))
                    ts(a, aring[:, n % 3, :], cact[:, 0:1], None, ALU.mult).then_inc(sem("ada_step"), 1)
                else:
                    stt(a, aring[:, n % 3, :], cact[:, c:c + 1], a, ALU.mult, ALU.add).then_inc(sem("ada_step"), 1)

            def mod(L):
                v.wait_ge(*full("mod", L + 1))
                tt(MOD[:, L, :], bank("mod", L)[:, 0:24], vecA[:, 24 * L:24 * L + 24], ALU.add
                   ).then_inc(drained["mod"], 1)
                v.wait_ge(*free("mod", L + 1))
                ts(MOD[:, L, 8:16], MOD[:, L, 8:16], 1.0, None, ALU.add).then_inc(sem("mod_ready"), 1)

            def rms(n, sums, count, width):
                v.wait_ge(sums, count)
                ts(ms[:, :], ss[:, :], 1.0 / width, EPS, ALU.mult, ALU.add).then_inc(sem("ms_ready"), 1)
                v.wait_ge(sem("rstd_ready"), n + 1)

            def normed(n):
                for b in range(NB):
                    ts(XN[:, b, :], X[:, b, :], rstd[:, b:b + 1], None, ALU.mult).then_inc(sem("xn"), 1)

            def hT(n, L):
                for c in range(0, KC, 2):
                    k = 4 * n + c // 2
                    v.wait_ge(*full("xTv", k + 1))
                    if c == 0:
                        v.wait_ge(sem("mod_ready"), L + 1)
                    ts(HT[:, c, :], bank("xTv", k), MOD[:, L, 8 + c:9 + c], MOD[:, L, c:c + 1], ALU.mult, ALU.add
                       ).then_inc(drained["xTv"], 1)

            def diag(k, L):
                if k == 0:
                    v.wait_ge(sem("rows_zero"), 16 * MAX_ITEMS)
                else:
                    v.wait_ge(*full("gate", 2 * k))
                for c in range(KC):
                    ts(DG[:, c, :], ident[:, :], MOD[:, L, 16 + c:17 + c], None, ALU.mult
                       ).then_inc(sem("diag"), 1)

            def residual(layer):
                v.wait_ge(*free("gate", 2 * (2 * layer + 1)))
                for n in range(8):
                    half, b = n // 4, n % 4
                    k = 8 * layer + n
                    v.wait_ge(*full("y", k + 1))
                    cols = slice(half * 512, half * 512 + 512)
                    tt(tmp[:, n % 2, :], bank("y", k), GB[:, cols], ALU.mult).then_inc(drained["y"], 1)
                    v.wait_ge(*free("y", k + 1))
                    tt(X[:, b, cols], X[:, b, cols], tmp[:, n % 2, :], ALU.add).then_inc(sem("x_done"), 1)

            for k, (dst, _) in enumerate(((vecA, VA), (vecB, VB))):
                v.wait_ge(*full("vec", k + 1))
                nc.vector.tensor_copy(dst[:, :], bank("vec", k)[:, 0:104]).then_inc(drained["vec"], 1)
            rms(0, sem("ss_ready"), 4, D)
            normed(0)
            masks(v, link)
            for m in range(2 * KC):
                ada(0, m)
            mod(0)
            hT(0, 0)
            step = [0]

            def one_ada(L):
                ada(L, step[0] % (2 * KC))
                step[0] += 1

            for f in range(4):
                v.wait_ge(*full("q", f + 1))
                ts(qT[:, f, :], bank("q", f), -(HD ** -0.5), None, ALU.mult).then_inc(drained["q"], 1)
                one_ada(1)
            for f in range(4):
                one_ada(1)
                v.wait_ge(*full("k", f + 1))
            for b in range(NB):
                v.wait_ge(*full("v", b + 1))
                nc.vector.tensor_copy(V0[:, b, :], bank("v", b)).then_inc(drained["v"], 1)
                one_ada(1)
            for b in range(NB):
                one_ada(1)
            mod(1)
            rms(1, sem("zss_ready"), 4, WA)
            v.wait_ge(sem("gz_in"), 16)
            for b in range(NB):
                stt(Z0[:, b, :], Z0[:, b, :], rstd[:, b:b + 1], gz, ALU.mult, ALU.mult).then_inc(sem("zn"), 1)

            for n in range(NB * NHA + 2):
                if n < NB * NHA:
                    i = n // NHA
                    cols = slice((NB - 1 - i) * P, S)
                    v.wait_ge(*full("score", n + 1))
                    if n >= 3:
                        v.wait_ge(*full("pT", n - 2))
                        v.wait_ge(sem("probs"), n - 2)
                    nc.vector.tensor_tensor_reduce(Pb[:, n % 3, 0:(i + 1) * P], bank("score", n)[:, 0:(i + 1) * P],
                                                   MA[:, cols], 1.0, 3e38, ALU.add, ALU.min, mx[:, n % 3:n % 3 + 1]
                                                   ).then_inc(drained["score"], 1)
                if 1 <= n <= NB * NHA:
                    m = n - 1
                    i = m // NHA
                    cols = slice((NB - 1 - i) * P, S)
                    v.wait_ge(sem("probs"), m + 1)
                    row = Pb[:, m % 3, 0:(i + 1) * P]
                    nc.vector.tensor_tensor_reduce(row, row, MU[:, cols], 1.0, 0.0, ALU.mult, ALU.add,
                                                   den[:, i % 2, m % NHA:m % NHA + 1]).then_inc(sem("pm"), 1)
                if n >= 2 and (n - 2) % NHA == NHA - 1:
                    i = (n - 2) // NHA
                    v.wait_ge(sem("pm"), NHA * (i + 1))
                    link(nc.vector.reciprocal(rden[:, i % 2, :], den[:, i % 2, :]))
                    v.wait_ge(sem("pv"), NHA * (i + 1))
                    if i >= 2:
                        v.wait_ge(*full("oT", i - 1))
                    tt(OB[:, i % 2, :].rearrange("p (h d) -> p h d", h=NHA),
                       bank("o", i).rearrange("p (h d) -> p h d", h=NHA),
                       rden[:, i % 2, :].unsqueeze(2).to_broadcast([P, NHA, HD]), ALU.mult
                       ).then_inc(drained["o"], 1)
                if n % 2 == 0 and step[0] < 32:
                    one_ada(2)
            for b in range(NB):
                v.wait_ge(*full("mix", b + 1))
                if b < 2:
                    v.wait_ge(*full("oT", 3 + b))
                else:
                    v.wait_ge(*full("sT", b - 1))
                g = lambda a: a.rearrange("p (h d) -> p h d", h=NHA)
                tt(g(OB[:, b % 2, :]), g(bank("mix", b)), bsT.unsqueeze(2).to_broadcast([P, NHA, HD]), ALU.add
                   ).then_inc(drained["mix"], 1)
                v.wait_ge(*free("mix", b + 1))
                v.wait_ge(*free("u", b + 1))
                tt(OB[:, b % 2, :], OB[:, b % 2, :], U0[:, b, :], ALU.mult).then_inc(sem("sgu_ob"), 1)
            mod(2)
            diag(0, 0)
            for m in range(2 * KC):
                ada(3, m)
            residual(0)
            mod(3)

            def moe(layer):
                M = lambda name: moe_sem(layer, name)
                L = 2 * layer + 1
                rms(2 + 2 * layer, sem("ss_ready"), 4 * (L + 1), D)
                normed(L)
                hT(L, L)
                diag(L, L)
                route(v, link, layer, M)
                n = v.value_load(CN[0:1, 0:1], min_val=8, max_val=MAX_ITEMS)

                def turned(wait):
                    v.wait_ge(M("tx"), wait)
                    for c in range(4, 8):
                        last = ts(XgT[:, c, :], PS[:, 1, (c - 4) * P:(c - 3) * P], MOD[:, L, 8 + c:9 + c],
                                  MOD[:, L, c:c + 1], ALU.mult, ALU.add)
                    last.then_inc(M("xgv"), 1)

                turned(1)
                v.wait_ge(*free("gate", 2 * (L + 1)))
                with v.Fori(0, n) as i:
                    v.wait_ge(M("sil"), i + 1)
                    v.wait_ge(M("up"), i + 1)
                    tt(hid, sil, PS[:, 2, DEXP:2 * DEXP], ALU.mult).then_inc(M("hid"), 1)
                    turned(i + 2)
                    v.wait_ge(M("th"), i + 1)
                    nc.vector.tensor_copy(hidT, PS[:, 4, 0:2 * P].rearrange("p (c t) -> p c t", c=2)
                                          ).then_inc(M("hT"), 1)
                    v.wait_ge(M("down"), i + 1)
                    v.wait_ge(M("row_out"), i * 16)
                    tt(Yt[:, 0:512], PS[:, 6, :], GB[:, 0:512], ALU.mult)
                    tt(Yt[:, 512:1024], PS[:, 7, :], GB[:, 512:1024], ALU.mult).then_inc(M("yt"), 1)
                nc.vector.engine_nop().then_inc(M("yt_last"), 1)
                for b in range(NB):
                    v.wait_ge(M(f"pair_in{b}"), 32)
                    for j in range(2):
                        if b or j:
                            v.wait_ge(sem("x_done"), 8 * L + 2 * b + j)
                        stt(X[:, b, :], CB[:, 2 * b + j, :], W12[:, j, b:b + 1], X[:, b, :], ALU.mult, ALU.add
                            ).then_inc(sem("x_done"), 1)

            moe(0)

            def rwkv():
                rms(3, sem("ss_ready"), 12, D)
                normed(2)
                hT(2, 2)
                low = tmp[:, :, :].rearrange("p a b -> p (a b)").bitcast(I32)
                xr, sh = low[:, 0:P], low[:, P:2 * P]
                link(nc.vector.tensor_copy(sh, io128[:, :]))
                link(ts(xr, ones[:, :], tid[:, 0:1], None, ALU.mult))
                link(tt(xr, xr, sh, ALU.bitwise_xor))
                link(ts(LV[:, :], xr, 0.0, None, ALU.is_gt))
                for lv in range(1, LEVELS + 1):
                    link(stt(LV[:, :], xr, float(2 ** lv), LV[:, :], ALU.is_ge, ALU.add))
                link(tt(LV[:, :], LV[:, :], upper[:, :], ALU.mult))
                for k in range(4):
                    if k % 2:
                        tt(MK[:, k * P:(k + 1) * P], upper[:, :], ident[:, :], ALU.add)
                    else:
                        nc.vector.tensor_copy(MK[:, k * P:(k + 1) * P], upper[:, :])
                ts(oka[:, :], vecB[:, 72:80], -1.0, 1.0, ALU.mult, ALU.add).then_inc(sem("levels"), 1)
                v.wait_ge(*free("xTa", 12))
                v.wait_ge(*free("xTv", 12))
                v.wait_ge(*full("xTa", 12))
                for c in range(KC):
                    tt(XX[:, c, 1:S], HT[:, c, 0:S - 1], HT[:, c, 1:S], ALU.subtract)
                    last = ts(XX[:, c, 0:1], HT[:, c, 0:1], -1.0, None, ALU.mult)
                link(last)
                used = {2: ("wl", 1), 3: ("al", 1), 4: ("gl", 2), 5: ("v1", 8)}
                for m, mu in enumerate((1, 4, 5, 3, 0, 2)):
                    if m in used:
                        k, n = used[m]
                        v.wait_ge(*full(k, n))
                    for c in range(KC):
                        stt(XM[m % 2][:, c, :], XX[:, c, :], vecB[:, mu * 8 + c:mu * 8 + c + 1], HT[:, c, :],
                            ALU.mult, ALU.add).then_inc(sem("mixed"), 1)
                for c in range(KC):
                    v.wait_ge(*full("k1", c + 1))
                    nc.vector.tensor_copy(K1[:, c, :], bank("k1", c)).then_inc(drained["k1"], 1)
                    v.wait_ge(*free("k1", c + 1))
                    ts(KK[:, c, :], K1[:, c, :], vecB[:, 64 + c:65 + c], None, ALU.mult).then_inc(sem("kkr"), 1)
                for c in range(KC):
                    v.wait_ge(*full("nrm", c + 1))
                    ts(RN[:, c, :], bank("nrm", c), 1e-24, None, ALU.max).then_inc(drained["nrm"], 1)
                    v.wait_ge(*free("nrm", c + 1))
                    nc.vector.reciprocal(RN[:, c, :], RN[:, c, :]).then_inc(sem("kinv"), 1)
                for c in range(KC):
                    v.wait_ge(sem("knorm"), c + 1)
                    v.wait_ge(sem("ksq"), c + 1)
                    v.wait_ge(*free("za", c + 1))
                    link(tt(KK[:, c, :], KK[:, c, :], RN[:, c, :], ALU.mult))
                    link(ts(tmp[:, 0, :], AA[:, c, :], vecB[:, 72 + c:73 + c], oka[:, c:c + 1], ALU.mult, ALU.add))
                    tt(K1[:, c, :], K1[:, c, :], tmp[:, 0, :], ALU.mult)
                    last = tt(AA[:, c, :], AA[:, c, :], KK[:, c, :], ALU.mult)
                link(last)
                num = {k: 0 for k in ("sc", "Tn", "Tt", "R", "dS")}

                def nxt(kind):
                    num[kind] += 1
                    return num[kind] - 1

                b4 = lambda a: a.rearrange("p (j t) -> p j t", j=NB)
                for step in scan_steps():
                    kind = step[0]
                    if kind == "prep":
                        c = step[1]
                        if c:
                            v.wait_ge(*full("bon", c))
                        else:
                            v.wait_ge(*free("zw", KC))
                        stt(tmp[:, 0, :], R1[:, c, :], vecB[:, 80 + c:81 + c], K1[:, c, :], ALU.mult, ALU.mult
                            ).then_inc(sem("rk"), 1)
                        if c:
                            v.wait_ge(sem("prep_done"), c)
                        link(nc.vector.tensor_tensor_scan(CU, NM[:, :], SGW[:, c, :], 0.0, ALU.mult, ALU.add))
                        link(nc.vector.tensor_copy(MID[:, :], CU[:, HD - 1:S:P]))
                        tt(b4(CU), b4(CU), MID[:, :].unsqueeze(2).to_broadcast([P, NB, P]), ALU.subtract
                           ).then_inc(sem("cc"), 1)
                        v.wait_ge(sem("cc"), c + 1)
                        tt(SGW[:, c, :], CU, SGW[:, c, :], ALU.subtract).then_inc(sem("ce"), 1)
                        v.wait_ge(sem("ee"), c + 1)
                        v.wait_ge(sem("e1"), c + 1)
                        link(tt(DD[:, c % 3, 0:NB - 1], EE[:, 0:NB - 1], EM[:, 1:NB], ALU.mult))
                        tt(R1[:, c, :], R1[:, c, :], E1, ALU.mult)
                        v.wait_ge(sem("e2"), c + 1)
                        stt(KK[:, c, :], KK[:, c, :], -1.0, SGW[:, c, :], ALU.mult, ALU.mult)
                        v.wait_ge(sem("e3"), c + 1)
                        tt(AA[:, c, :], AA[:, c, :], CU, ALU.mult)
                        tt(K1[:, c, :], K1[:, c, :], CU, ALU.mult).then_inc(sem("prep_done"), 1)
                    elif kind == "turn":
                        c = step[1]
                        v.wait_ge(*full("bon", c + 1))
                        nc.vector.tensor_copy(BON[:, c, :], bank("bon", c)[:, 0:8]).then_inc(drained["bon"], 1)
                        v.wait_ge(*free("bon", c + 1))
                    elif kind == "scores":
                        _, c, h, j = step
                        n = nxt("sc")
                        v.wait_ge(*full("sc", n + 1))
                        if n == 0:
                            v.wait_ge(sem("zeroed"), 2)
                        if c >= 1:
                            v.wait_ge(*full("X", 2 * LEVELS * c))
                            v.wait_ge(sem("lm_ready"), 2 * LEVELS * c)
                        ps = bank("sc", n)
                        nc.vector.copy_predicated(LT[h][:, j, :], MK[:, 0:P], ps[:, 0:P]).then_inc(sem("lt_ready"), 1)
                        if c >= 2:
                            v.wait_ge(*full("Y", 8 * (c - 1)))
                        nc.vector.copy_predicated(PM[c % 2][h][:, j, :, :].rearrange("p m t -> p (m t)"),
                                                  MK[:, P:4 * P], ps[:, P:4 * P]).then_inc(drained["sc"], 1)
                    elif kind == "T":
                        _, c, h, lv = step
                        if lv < LEVELS - 1:
                            n = nxt("Tn")
                            v.wait_ge(*full("Tn", n + 1))
                            if lv == 0:
                                v.wait_ge(*free("lo", 2 * c + h + 1))
                            tt(Tn[h], Tn[h], b4(bank("Tn", n)), ALU.add).then_inc(drained["Tn"], 1)
                        n = nxt("Tt")
                        v.wait_ge(*full("Tt", n + 1))
                        if lv == 0:
                            v.wait_ge(sem("tt0"), 2 * c + h + 1)
                        tt(Tt[c % 2][h], Tt[c % 2][h], b4(bank("Tt", n)), ALU.add).then_inc(drained["Tt"], 1)
                    elif kind == "R":
                        _, c, h, j = step
                        n = nxt("R")
                        v.wait_ge(*full("R", n + 1))
                        if n >= 2:
                            v.wait_ge(*full("U", n - 1))
                        nc.vector.tensor_copy(RH[:, h, :], bank("R", n)[:, 0:HD]).then_inc(drained["R"], 1)
                    elif kind == "dS":
                        _, c, h, j = step
                        n = nxt("dS")
                        lo = slice(h * HD, (h + 1) * HD)
                        d = DD[lo, c % 3, j:j + 1]
                        ps = bank("dS", n)[lo, 0:HD]
                        new = ST[lo, (j + 1) % 2, :]
                        v.wait_ge(sem("prep_done"), c + 1)
                        if j == 0:
                            v.wait_ge(*full("dS", n + 1))
                            if c:
                                v.wait_ge(*full("Y", 8 * c))
                            ts(new, ps, d, None, ALU.mult).then_inc(drained["dS"], 1)
                        else:
                            v.wait_ge(*free("dS", n - 1))
                            link(ts(SD[lo, :], ST[lo, j % 2, :], d, None, ALU.mult))
                            v.wait_ge(*full("dS", n + 1))
                            stt(new, ps, d, SD[lo, :], ALU.mult, ALU.add).then_inc(drained["dS"], 1)
                    elif kind == "norm":
                        c = step[1]
                        y = SGW[:, c, :].rearrange("p (n d) -> p n d", d=HD)
                        v.wait_ge(*free("Y", 8 * (c + 1)))
                        link(red(sm[:, 0, :], y, AX, ALU.add))
                        link(ts(sm[:, 1, :], sm[:, 0, :], 1.0 / HD, None, ALU.mult))
                        tt(y, y, sm[:, 1, :].unsqueeze(2).to_broadcast([P, 8, HD]), ALU.subtract
                           ).then_inc(sem("gn_mean"), 1)
                        v3 = V1[:, :, c * P:(c + 1) * P]
                        for j in range(NB):
                            last = tt(v3[:, j, :].rearrange("p (h d) -> p h d", h=2),
                                      v3[:, j, :].rearrange("p (h d) -> p h d", h=2),
                                      BON[:, c, 2 * j:2 * j + 2].unsqueeze(2).to_broadcast([P, 2, HD]), ALU.mult)
                        last.then_inc(sem("gn_bv"), 1)
                        v.wait_ge(sem("gn_sq"), c + 1)
                        link(red(sm[:, 0, :], KK[:, c, :].rearrange("p (n d) -> p n d", d=HD), AX, ALU.add))
                        ts(sm[:, 2, :], sm[:, 0, :], 1.0 / HD, GN_EPS, ALU.mult, ALU.add).then_inc(sem("gn_var"), 1)
                        v.wait_ge(sem("gn_rstd"), c + 1)
                        tt(y, y, sm[:, 3, :].unsqueeze(2).to_broadcast([P, 8, HD]), ALU.mult).then_inc(sem("gn_y"), 1)
                for k in range(8):
                    half, b = k // 4, k % 4
                    v.wait_ge(*full("g", k + 1))
                    if k == 0:
                        v.wait_ge(sem("y_ready"), KC)
                    cols = slice(half * 512, half * 512 + 512)
                    tt(V1[:, b, cols], V1[:, b, cols], bank("g", k), ALU.mult).then_inc(drained["g"], 1)
                v.wait_ge(*full("g", 8))
                diag(2, 2)
                residual(1)

            rwkv()
            moe(1)
            rms(5, sem("ss_ready"), 20, D)
            normed(4)
            v.wait_ge(sem("fin_in"), 16)
            for b in range(NB):
                v.wait_ge(sem("xn"), 17 + b)
                tt(XN[:, b, :], XN[:, b, :], LNW, ALU.mult).then_inc(sem("fin"), 1)

        @block.tensor
        def _(pe):
            mm = nc.tensor.matmul

            def norm_T(n):
                for c in range(KC):
                    kind = "xTa" if c % 2 else "xTv"
                    k = 4 * n + c // 2
                    out = open_bank(pe, kind, k)
                    if c == 0:
                        pe.wait_ge(sem("xn"), NB * (n + 1))
                    for b in range(NB):
                        last = nc.tensor.transpose(out[:, b * P:(b + 1) * P], XN[:, b, c * P:(c + 1) * P], ident[:, :])
                    last.then_inc(filled[kind], 1)

            def mod(L):
                out = open_bank(pe, "mod", L)
                pe.wait_ge(sem("ada_step"), 2 * KC * (L + 1))
                for j in range(24):
                    last = mm(out[:, j:j + 1], acc[:, j * P:(j + 1) * P], ones[:, 0:1], start=True, stop=True)
                last.then_inc(filled["mod"], 1)

            def gate(k):
                for half in range(2):
                    out = open_bank(pe, "gate", 2 * k + half)
                    pe.wait_ge(sem("diag"), 8 * k + 4 * half + 4)
                    for c in range(4):
                        last = mm(out[:, c * P:(c + 1) * P], ones[:, :], DG[:, 4 * half + c, :], start=True, stop=True)
                    last.then_inc(filled["gate"], 1)

            def rows(kind, k, b, tile, act_T):
                out = open_bank(pe, kind, k)
                for c in range(KC):
                    last = mm(out, act_T[:, c, b * P:(b + 1) * P], WR[:, tile % 2, c, :], start=(c == 0),
                              stop=(c == KC - 1))
                last.then_inc(filled[kind], 1)

            def feats(kind, k, f, tile, act_T):
                out = open_bank(pe, kind, k)
                for c in range(KC):
                    last = mm(out, WR[:, tile % 2, c, f * P:(f + 1) * P], act_T[:, c, :], start=(c == 0),
                              stop=(c == KC - 1))
                last.then_inc(filled[kind], 1)

            def hT_ready(n):
                pe.wait_ge(*free("xTv", 4 * (n + 1)))
                pe.wait_ge(*free("xTa", 4 * (n + 1)))

            def out_proj(layer, first_tile):
                for half in range(2):
                    tile_ready(pe, first_tile + half)
                    for b in range(NB):
                        rows("y", 8 * layer + 4 * half + b, b, first_tile + half, HT)

            pe.wait_ge(sem("ident_ready"), 1)
            pe.wait_ge(sem("vec_in"), 16 * 10)
            for k, r in enumerate((VA, VB)):
                out = open_bank(pe, "vec", k)
                nc.tensor.transpose(out[:, 0:104], r[0:104, :], ident[0:104, 0:104]).then_inc(filled["vec"], 1)
            pe.wait_ge(sem("ones_ready"), 1)
            mod(0)
            norm_T(0)
            hT_ready(0)
            for n, kind in enumerate(("q", "k")):
                tile_ready(pe, n)
                for f in range(4):
                    feats(kind, f, f, n, HT)
            for n, kind in enumerate(("v", "u", "z")):
                tile_ready(pe, 2 + n)
                for b in range(NB):
                    rows(kind, b, b, 2 + n, HT)
            mod(1)
            pe.wait_ge(*free("q", 4))
            pe.wait_ge(*free("k", 4))
            pe.wait_ge(*free("v", 4))
            for n in range(NB * NHA + 2):
                if n < NB * NHA:
                    i, h = n // NHA, n % NHA
                    lo = HD * (h % 2)
                    out = open_bank(pe, "score", n)
                    if n == 0:
                        pe.wait_ge(sem("zss_ready"), 4)
                    mm(out[:, 0:(i + 1) * P], qT[lo:lo + HD, h // 2, i * P:(i + 1) * P],
                       kT[lo:lo + HD, h // 2, 0:(i + 1) * P], start=True, stop=True).then_inc(filled["score"], 1)
                if 1 <= n <= NB * NHA:
                    m = n - 1
                    i = m // NHA
                    out = open_bank(pe, "pT", m)
                    pe.wait_ge(sem("pm"), m + 1)
                    for j in range(i + 1):
                        last = nc.tensor.transpose(out[:, j * P:(j + 1) * P], Pb[:, m % 3, j * P:(j + 1) * P],
                                                   ident[:, :])
                    last.then_inc(filled["pT"], 1)
                if n >= 2:
                    m = n - 2
                    i, h = m // NHA, m % NHA
                    out = open_bank(pe, "o", i) if h == 0 else bank("o", i)
                    pe.wait_ge(*free("pT", m + 1))
                    for j in range(i + 1):
                        last = mm(out[:, h * HD:(h + 1) * HD], PT[:, m % 3, j * P:(j + 1) * P],
                                  V0[:, j, h * HD:(h + 1) * HD], start=(j == 0), stop=(j == i))
                    last.then_inc(sem("pv"), 1)
                    if h == NHA - 1:
                        out = open_bank(pe, "oT", i)
                        pe.wait_ge(*free("o", i + 1))
                        for c in range(4):
                            last = nc.tensor.transpose(out[:, c * P:(c + 1) * P], OB[:, i % 2, c * P:(c + 1) * P],
                                                       ident[:, :])
                        last.then_inc(filled["oT"], 1)
            pe.wait_ge(sem("swm"), 1)
            for k in range(2):
                out = open_bank(pe, "swT", k)
                for c in range(4):
                    last = nc.tensor.transpose(out[:, c * P:(c + 1) * P], SW[:, 4 * k + c, :], ident[:, :])
                last.then_inc(filled["swT"], 1)
            for b in range(NB):
                out = open_bank(pe, "mix", b)
                pe.wait_ge(*free("swT", 2))
                pe.wait_ge(sem("zn"), b + 1)
                for g in range(NHA):
                    last = mm(out[:, g * HD:(g + 1) * HD], SWT[:, g, :], Z0[:, b, g * HD:(g + 1) * HD],
                              start=True, stop=True)
                last.then_inc(filled["mix"], 1)
            for b in range(NB):
                out = open_bank(pe, "sT", b)
                pe.wait_ge(sem("sgu_ob"), b + 1)
                for c in range(4):
                    last = nc.tensor.transpose(out[:, c * P:(c + 1) * P], OB[:, b % 2, c * P:(c + 1) * P], ident[:, :])
                last.then_inc(filled["sT"], 1)
            mod(2)
            gate(0)
            pe.wait_ge(*free("oT", 4))
            pe.wait_ge(*free("sT", 4))
            out_proj(0, 5)
            mod(3)

            def moe(layer):
                M = lambda name: moe_sem(layer, name)
                L = 2 * layer + 1
                norm_T(L)
                hT_ready(L)
                pe.wait_ge(sem("rw_in"), 16)
                out = open_bank(pe, "logit", layer)
                for b in range(NB):
                    for c in range(KC):
                        last = mm(out[:, b * NEXP:(b + 1) * NEXP], HT[:, c, b * P:(b + 1) * P], RWt[:, c, :],
                                  start=(c == 0), stop=(c == KC - 1))
                last.then_inc(filled["logit"], 1)
                out = open_bank(pe, "rank", layer)
                pe.wait_ge(M("chosen"), 1)
                pe.wait_ge(sem("moe_consts"), 4)
                for b in range(NB):
                    for k in range(b + 1):
                        mm(out[:, b * NEXP:(b + 1) * NEXP], upper[:, :] if k == b else ones[:, :], CH[:, k, :],
                           start=(k == 0), stop=(k == b))
                for k in range(NB):
                    last = mm(out[:, 64:64 + NEXP], ones[:, :], CH[:, k, :], start=(k == 0), stop=(k == NB - 1))
                last.then_inc(filled["rank"], 1)
                out = open_bank(pe, "list", layer)
                pe.wait_ge(M("hot"), 1)
                for k in range(8):
                    last = mm(out[:, 0:25], HOTR[:, k, :], HOTI[:, k, :], start=(k == 0), stop=(k == 7))
                last.then_inc(filled["list"], 1)
                gate(L)
                for kind in ("gate", "list", "rank", "logit", "xTa", "xTv"):
                    pe.wait_ge(*free(kind, {"gate": 2 * (L + 1), "list": layer + 1, "rank": layer + 1,
                                               "logit": layer + 1, "xTa": 4 * (L + 1), "xTv": 4 * (L + 1)}[kind]))
                pe.wait_ge(M("items"), 1)
                n = pe.value_load(CN[0:1, 0:1], min_val=8, max_val=MAX_ITEMS)

                def turn(wait):
                    pe.wait_ge(M("xg_in"), wait)
                    for c in range(KC):
                        last = nc.tensor.transpose(PS[:, c // 4, (c % 4) * P:(c % 4 + 1) * P],
                                                   Xg[:, c * P:(c + 1) * P], ident[:, :])
                    last.then_inc(M("tx"), 1)

                turn(16)
                with pe.Fori(0, n) as i:
                    slot = bass.ds(i % 2, 1)
                    pe.wait_ge(M("xga"), i + 1)
                    pe.wait_ge(M("xgv"), i + 1)
                    pe.wait_ge(M("w1_in"), i * 16 + 16)
                    pe.wait_ge(M("w3_in"), i * 16 + 16)
                    pe.wait_ge(M("hid"), i)
                    for c in range(KC):
                        last = mm(PS[:, 2, :], XgT[:, c, :],
                                  WR[:, slot, c, :].rearrange("p s f -> p (s f)"),
                                  start=(c == 0), stop=(c == KC - 1))
                    last.then_inc(M("up"), 1)
                    turn(i * 16 + 32)
                    pe.wait_ge(M("hid"), i + 1)
                    for c in range(2):
                        last = nc.tensor.transpose(PS[:, 4, c * P:(c + 1) * P], hid[:, c * P:(c + 1) * P], ident[:, :])
                    last.then_inc(M("th"), 1)
                    pe.wait_ge(M("hT"), i + 1)
                    pe.wait_ge(M("w2_in"), i * 16 + 16)
                    pe.wait_ge(M("yt"), i)
                    for half in range(2):
                        for c in range(2):
                            last = mm(PS[:, 6 + half, :], hidT[:, c, :],
                                      W2[:, slot, c, half * 512:half * 512 + 512].rearrange("p s f -> p (s f)"),
                                      start=(c == 0), stop=(c == 1))
                    last.then_inc(M("down"), 1)

            moe(0)

            def rwkv():
                pe.wait_ge(moe_sem(0, "yt_last"), 1)
                norm_T(2)
                pe.wait_ge(sem("lora_in"), 48)

                def small(kind, k, out, w, x, m):
                    for c in range(KC):
                        if k == 0:
                            pe.wait_ge(sem("mixed"), 8 * m + c + 1)
                        last = mm(out, w[:, c, :], x[:, c, :], start=(c == 0), stop=(c == KC - 1))
                    last.then_inc(filled[kind], 1)

                small("wl", 0, open_bank(pe, "wl", 0)[0:HD, :], W1L, XM[0], 0)
                small("al", 0, open_bank(pe, "al", 0)[HD:P, :], A1L, XM[1], 1)
                small("gl", 0, open_bank(pe, "gl", 0), G1L[:, :, 0:P], XM[0], 2)
                small("gl", 1, open_bank(pe, "gl", 1)[0:32, :], G1L[:, :, P:P + 32], XM[0], 2)
                pe.wait_ge(sem("mixed"), 32)
                for k in range(8):
                    if k % 4 == 0:
                        tile_ready(pe, 7 + k // 4)
                    rows("v1", k, k % 4, 7 + k // 4, XM[1])
                for kind, first, x, m in (("r1", 9, XM[0], 5), ("k1", 11, XM[1], 6)):
                    pe.wait_ge(sem("mixed"), 8 * m)
                    for k in range(8):
                        if k % 4 == 0:
                            tile_ready(pe, first + k // 4)
                        feats(kind, k, k % 4, first + k // 4, x)
                pe.wait_ge(sem("wa2_in"), 32)
                pe.wait_ge(sem("blk_ready"), 2)
                pe.wait_ge(*free("wl", 1))
                pe.wait_ge(*free("al", 1))
                for c in range(KC):
                    mm(open_bank(pe, "zw", c), WA2[0:HD, c * P:(c + 1) * P], TWA[0:HD, :], start=True, stop=True
                       ).then_inc(filled["zw"], 1)
                    mm(open_bank(pe, "za", c), WA2[HD:P, c * P:(c + 1) * P], TWA[HD:P, :], start=True, stop=True
                       ).then_inc(filled["za"], 1)
                    out = open_bank(pe, "nrm", c)
                    pe.wait_ge(sem("ksq"), c + 1)
                    mm(out, blk[:, :], (CU, E1)[c % 2], start=True, stop=True).then_inc(filled["nrm"], 1)
                num = {k: 0 for k in ("sc", "X", "Tn", "Tt", "R", "U", "Y", "dS")}

                def nxt(kind):
                    num[kind] += 1
                    return num[kind] - 1

                for step in scan_steps():
                    kind = step[0]
                    if kind == "turn":
                        c = step[1]
                        pe.wait_ge(sem("prep_done"), c + 1)
                        for g in range(2):
                            out = open_bank(pe, "bkT", 2 * c + g)
                            for q in range(4):
                                j, x = 2 * g + q // 2, (AA, K1)[q % 2]
                                last = nc.tensor.transpose(out[:, q * P:(q + 1) * P], x[:, c, j * P:(j + 1) * P],
                                                           ident[:, :])
                            last.then_inc(filled["bkT"], 1)
                        out = open_bank(pe, "bon", c)
                        pe.wait_ge(sem("rk"), c + 1)
                        for j in range(NB):
                            last = mm(out[:, 2 * j:2 * j + 2], tmp[:, 0, j * P:(j + 1) * P], blk[:, 0:P:HD],
                                      start=True, stop=True)
                        last.then_inc(filled["bon"], 1)
                    elif kind == "scores":
                        _, c, h, j = step
                        n = nxt("sc")
                        lo = slice(h * HD, (h + 1) * HD)
                        at = slice(c * S + j * P, c * S + (j + 1) * P)
                        out = open_bank(pe, "sc", n)
                        for m, left in enumerate((4, 7)):
                            last = mm(out[:, m * 256:(m + 1) * 256].rearrange("p (a t) -> p a t", a=2),
                                      arena[lo, left, at], arena[lo, 2:7:4, at], start=True, stop=True)
                        last.then_inc(filled["sc"], 1)
                    elif kind == "lower":
                        _, c, h = step
                        out = open_bank(pe, "lo", 2 * c + h)
                        pe.wait_ge(sem("tt0"), 2 * c + h + 1)
                        for j in range(NB):
                            last = nc.tensor.transpose(out[:, j * P:(j + 1) * P], Tt[c % 2][h][:, j, :], ident[:, :])
                        last.then_inc(filled["lo"], 1)
                    elif kind == "X":
                        _, c, h, lv = step
                        n = nxt("X")
                        out = open_bank(pe, "X", n)
                        pe.wait_ge(sem("lm_ready"), n + 1)
                        if lv == 0:
                            pe.wait_ge(*free("lo", 2 * c + h + 1))
                        else:
                            pe.wait_ge(*free("Tn", 2 * (LEVELS - 1) * c + 2 * (lv - 1) + h + 1))
                        for j in range(NB):
                            last = mm(out[:, j * P:(j + 1) * P], LM[h][:, j, :], Tn[h][:, j, :], start=True, stop=True)
                        last.then_inc(filled["X"], 1)
                    elif kind == "T":
                        _, c, h, lv = step
                        pe.wait_ge(*free("X", 2 * LEVELS * c + 2 * lv + h + 1))
                        if lv:
                            pe.wait_ge(*free("Tt", 2 * LEVELS * c + 2 * (lv - 1) + h + 1))
                        if lv < LEVELS - 1:
                            n = nxt("Tn")
                            out = open_bank(pe, "Tn", n)
                            for j in range(NB):
                                last = mm(out[:, j * P:(j + 1) * P], Tt[c % 2][h][:, j, :], XT[h][:, j, :],
                                          start=True, stop=True)
                            last.then_inc(filled["Tn"], 1)
                        n = nxt("Tt")
                        out = open_bank(pe, "Tt", n)
                        for j in range(NB):
                            last = mm(out[:, j * P:(j + 1) * P], XT[h][:, j, :], Tt[c % 2][h][:, j, :],
                                      start=True, stop=True)
                        last.then_inc(filled["Tt"], 1)
                    elif kind in ("R", "U", "Y", "dS"):
                        _, c, h, j = step
                        n = nxt(kind)
                        head = slice((2 * c + h) * HD, (2 * c + h + 1) * HD)
                        lo = slice(h * HD, (h + 1) * HD)
                        V = V1[:, j, head]
                        pm = PM[c % 2][h]
                        at = slice(j * P, (j + 1) * P)
                        st = ST[lo, j % 2, :]
                        out = open_bank(pe, kind, n)
                        if kind == "R":
                            if j:
                                pe.wait_ge(*free("dS", 6 * c + 2 * (j - 1) + h + 1))
                            else:
                                pe.wait_ge(*free("sc", 8 * c + 4 * (h + 1)))
                            last = mm(out[:, 0:HD], pm[:, j, 1, :], V, start=True, stop=(j == 0))
                            if j:
                                last = mm(out[:, 0:HD], KK[lo, c, at], st, start=False, stop=True)
                            last.then_inc(filled["R"], 1)
                        elif kind == "U":
                            pe.wait_ge(*free("R", 8 * c + 2 * j + h + 1))
                            pe.wait_ge(*free("Tt", 2 * LEVELS * (c + 1)))
                            mm(out[:, 0:HD], Tt[c % 2][h][:, j, :], RH[:, h, :], start=True, stop=True
                               ).then_inc(filled["U"], 1)
                        elif kind == "Y":
                            mm(out[:, 0:HD], pm[:, j, 2, :], V, start=True, stop=False)
                            if j:
                                mm(out[:, 0:HD], R1[lo, c, at], st, start=False, stop=False)
                            pe.wait_ge(*free("U", 8 * c + 2 * j + h + 1))
                            mm(out[:, 0:HD], pm[:, j, 0, :], UU[:, h, :], start=False, stop=True
                               ).then_inc(filled["Y"], 1)
                        else:
                            pe.wait_ge(*free("bkT", 2 * (c + 1)))
                            mm(out[lo, 0:HD], BK[c % 2][:, j, 1, lo], V, start=True, stop=False)
                            mm(out[lo, 0:HD], BK[c % 2][:, j, 0, lo], UU[:, h, :], start=False, stop=True
                               ).then_inc(filled["dS"], 1)
                pe.wait_ge(sem("g2_in"), 32)
                for k in range(8):
                    half, b = k // 4, k % 4
                    out = open_bank(pe, "g", k)
                    cols = slice(half * 512, half * 512 + 512)
                    at = slice(b * P, (b + 1) * P)
                    mm(out, TG[:, 0, at], G2A[:, cols], start=True, stop=False)
                    mm(out, TG[0:32, 1, at], G2B[:, cols], start=False, stop=True).then_inc(filled["g"], 1)
                for c in range(KC):
                    out = open_bank(pe, "yT", c)
                    pe.wait_ge(*free("g", 4 * (c // 4) + 4))
                    for b in range(NB):
                        last = nc.tensor.transpose(out[:, b * P:(b + 1) * P], V1[:, b, c * P:(c + 1) * P], ident[:, :])
                    last.then_inc(filled["yT"], 1)
                gate(2)
                pe.wait_ge(*free("yT", 8))
                out_proj(1, 13)

            rwkv()
            moe(1)

    return nc


_INS = ['x', 'c', 'ada_w', 'ada_b', 'mix_w_in', 'mix_w_out', 'sgu_norm_g', 'sgu_w', 'sgu_b',
        'rwkv_mu', 'rwkv_w_rkv', 'rwkv_w_o', 'rwkv_w0', 'rwkv_w1', 'rwkv_w2', 'rwkv_a0', 'rwkv_a1', 'rwkv_a2',
        'rwkv_g1', 'rwkv_g2', 'rwkv_k_k', 'rwkv_k_a', 'rwkv_r_k', 'rwkv_ln_w', 'rwkv_ln_b',
        'router_w', 'router_b', 'moe_w1', 'moe_w3', 'moe_w2', 'final_norm_g']


def kernel(**inputs):
    import numpy as np
    import concourse.bacc as bacc
    from concourse.bass_utils import run_bass_kernel_spmd

    nc = bacc.Bacc("TRN2", target_bir_lowering=False, num_devices=1)
    arrays, io = {}, {}
    for name in _INS:
        a = np.ascontiguousarray(inputs[name])
        arrays[f"in_{name}"] = a
        io[name] = nc.dram_tensor(f"in_{name}", a.shape, mybir.dt.from_np(a.dtype), kind="ExternalInput").ap()
    io["out"] = nc.dram_tensor("out", (1, S, D), F32, kind="ExternalOutput").ap()
    build(nc, io)
    r = run_bass_kernel_spmd(nc, [arrays], core_ids=[0])
    return r.results[0]["out"]
```

```python
from contextlib import ExitStack

import concourse.bass as bass
from concourse import mybir
from concourse.alu_op_type import AluOpType as ALU

F32 = mybir.dt.float32
I32 = mybir.dt.int32
ACT = mybir.ActivationFunctionType
AX = mybir.AxisListType.X

P = 128
D = 1024
S = 512
NB = S // P
KC = D // P
HD = 64
NHA = 8
WA = NHA * HD
NEXP, NGRP, EPG, DEXP = 16, 4, 4, 256
NADA = 4
SPAN = 128
EPS = 1e-6
GN_EPS = 64e-5
KAPPA = float(2.718281828459045 ** -0.5)
NEG = 1e30
MAX_ITEMS = 24
RING = 6
LONG = 2


def bank_plan():
    plan, count = [], {}

    def add(kind, ring="a"):
        plan.append((kind, count.get(kind, 0), ring))
        count[kind] = count.get(kind, 0) + 1

    def norm():
        for c in range(KC):
            add("xTa" if c % 2 else "xTv")

    add("vec")
    add("vec")
    norm()
    add("mod")
    for kind in ("q", "k", "v", "u", "z"):
        for _ in range(4):
            add(kind)
        if kind == "k":
            add("mod")
    add("mod")
    for n in range(NB * NHA + 3):
        if n < NB * NHA:
            add("score")
        if n >= 2 and n - 2 < NB * NHA:
            add("pT")
        if n >= 3:
            if (n - 3) % NHA == 0:
                add("o", "b")
        if n >= 3 and (n - 3) % NHA == NHA - 1:
            add("oT")
    add("swT")
    add("swT")
    for b in range(NB):
        add("mix")
    for b in range(NB):
        add("sT")
    add("mod")
    for layer in range(2):
        if layer == 1:
            norm()
            rwkv_plan(add)
        add("gate")
        add("gate")
        for _ in range(2 * NB):
            add("y")
        if layer == 0:
            add("mod")
        norm()
        add("logit")
        add("rank")
        add("list")
        add("gate")
        add("gate")
    return plan


def rwkv_plan(add):
    for _ in range(8):
        add("v1")
    add("wl")
    add("al")
    add("gl")
    add("gl")
    for _ in range(8):
        add("r1")
    for c in range(KC + 1):
        if c < KC:
            add("k1")
            add("zw")
            add("za")
        if c:
            add("nrm")
    for step in scan_steps():
        kind = step[0]
        if kind == "turn":
            add("bkT")
            add("bkT")
            add("bon")
        elif kind == "scores":
            add("sc")
        elif kind == "lower":
            add("lo")
        elif kind == "X":
            add("X")
        elif kind == "T":
            add("Tt")
        elif kind == "N":
            add("Tn")
        elif kind in ("R", "U", "Y", "dS"):
            add(kind)
    for _ in range(2 * NB):
        add("g")
    for _ in range(KC):
        add("yT")


LEVELS = 6


WALKS = ((0, 1, 0, 1, 0, 1, 0, 1, 1), (0, 0, 0, 0, 0, 1), (1, 1, 1, 1, 1, 1), (1, 0, 1, 0, 0))


def scan_steps():
    steps = [("cumulate", 0), ("exponents", 0), ("exponents2", 0), ("scale", 0), ("place", 0)]
    for c in range(KC + 2):
        walk = []
        if 1 <= c <= KC:
            for j in range(NB):
                walk += [[("R", c - 1, h, j) for h in range(2)],
                         [("U", c - 1, h, j) for h in range(2)],
                         [("Y", c - 1, h, j) for h in range(2)]
                         + [("dS", c - 1, h, j) for h in range(2) if j < NB - 1]]
        norm = [(k, c - 2) for k in ("mean", "square", "variance", "rstd", "no step", "output") if c >= 2]
        ahead = [(k, c + 1) for k in ("cumulate", "exponents", "exponents2", "scale", "place") if c + 1 < KC]

        def take(queue, steps=steps):
            if queue:
                steps += queue.pop(0) if queue is walk else [queue.pop(0)]

        if c < KC:
            steps.append(("turn", c))
            for h in range(2):
                for j in range(NB):
                    steps.append(("scores", c, h, j))
                    if WALKS[0][4 * h + j]:
                        take(walk)
            for h in range(2):
                steps.append(("lower", c, h))
            if WALKS[0][8]:
                take(walk)
            take(norm)
            for lv in range(LEVELS):
                steps += [("X", c, h, lv) for h in range(2)]
                take(norm)
                if WALKS[1][lv]:
                    take(walk)
                steps += [("T", c, h, lv) for h in range(2)]
                if WALKS[2][lv]:
                    take(walk)
                if lv < LEVELS - 1:
                    steps += [("N", c, h, lv) for h in range(2)]
                    if WALKS[3][lv]:
                        take(walk)
                take(ahead)
        while walk:
            take(walk)
        while norm:
            take(norm)
    return steps


FILLED_TOGETHER = {
    "xT": ("xTa", "xTv"), "mod": ("vec", "mod"), "mixer_in": ("q", "k", "v", "u", "z"),
    "attention": ("score", "pT", "oT"), "gating": ("swT", "mix", "sT"),
    "rwkv_in": ("wl", "al", "gl", "v1", "r1", "k1", "zw", "za", "nrm"),
    "triangles": ("bkT", "bon", "sc", "lo", "X", "Tn", "Tt"), "walk": ("R", "U", "Y", "dS"), "rwkv_out": ("g", "yT"),
    "route": ("logit", "rank", "list"), "y": ("y",), "gate": ("gate",), "o": ("o",)}
EMPTIED_TOGETHER = {
    "mod_dve": ("vec", "mod"), "xT_act": ("xTa",), "xT_dve": ("xTv",), "mixer_in_act": ("k", "u", "z"),
    "mixer_in_dve": ("q", "v"), "mixer_act": ("pT", "oT", "swT", "sT"), "mixer_dve": ("score", "mix"), "o_dve": ("o",),
    "rwkv_in_act": ("wl", "al", "gl", "v1", "r1", "zw", "za"), "rwkv_in_dve": ("k1", "nrm"),
    "scan_act": ("bkT", "lo", "X", "Tn", "U", "Y"), "scan_dve": ("bon", "sc", "Tt", "R", "dS"),
    "y_dve": ("g", "y"), "gate_act": ("yT", "gate", "logit"), "route_dve": ("rank", "list")}


def shared(plan, families, what, sem):
    sems, value = {}, {}
    for family, kinds in families.items():
        count = 0
        for kind, n, _ in plan:
            if kind in kinds:
                count += 1
                value[kind, n + 1] = count
                sems[kind] = sem(f"{family}_{what}")
    return sems, lambda kind, n: (sems[kind], value[kind, n])


def build(nc, io):
    ctx = ExitStack()
    with ctx:
        def sb(name, shape, dt=F32):
            return ctx.enter_context(nc.sbuf_tensor(name, shape, dt))

        sems = {}

        def sem(name):
            if name not in sems:
                sems[name] = ctx.enter_context(nc.semaphore(name))
            return sems[name]

        arena = sb("arena", [P, 8, 4096])

        def area(i, pattern=None, **kw):
            a = arena[:, i, :]
            return a.rearrange(pattern, **kw) if pattern else a

        X = area(0, "p (b f) -> p b f", b=NB)
        HT = area(1, "p (c t) -> p c t", c=KC)
        XN = area(2, "p (b f) -> p b f", b=NB)
        qT = arena[:, 3, 0:2048].rearrange("p (f t) -> p f t", f=4)
        kT = arena[:, 3, 2048:4096].rearrange("p (f t) -> p f t", f=4)
        V0 = arena[:, 4, 0:2048].rearrange("p (b f) -> p b f", b=NB)
        U0 = arena[:, 4, 2048:4096].rearrange("p (b f) -> p b f", b=NB)
        Z0 = arena[:, 5, 0:2048].rearrange("p (b f) -> p b f", b=NB)
        SW = arena[:, 5, 2048:3072].rearrange("p (g j) -> p g j", g=NHA)
        SWT = arena[:, 5, 3072:4096].rearrange("p (g j) -> p g j", g=NHA)
        Pb = arena[:, 2, 0:1536].rearrange("p (n s) -> p n s", n=3)
        PT = arena[:, 2, 1536:3072].rearrange("p (n s) -> p n s", n=3)
        OB = arena[:, 2, 3072:4096].rearrange("p (n s) -> p n s", n=2)
        acc = arena[:, 6:8, :].rearrange("p a n -> p (a n)")[:, 0:3072]
        aring = arena[:, 6:8, :].rearrange("p a n -> p (a n)")[:, 3072:7168].rearrange("p (n f) -> p n f", n=4)
        gz = arena[:, 6:8, :].rearrange("p a n -> p (a n)")[:, 7680:8192]
        WR = sb("WR", [P, 2, KC, 512])
        W2 = sb("W2", [P, 2, 2, D])
        LO = sb("LO", [P, 2304])
        TWA2 = sb("TWA2", [P, 2 * S])
        TWA = TWA2[:, 0:S]
        TG = sb("TG", [P, 2, S])


        ident = sb("ident", [P, P])
        ones = sb("ones", [P, P])
        blk = sb("blk", [P, P])
        upper = sb("upper", [P, P])
        w2flat = W2[:, :, :, :].rearrange("p a b c -> p (a b c)")
        MA = w2flat[:, 0:512]
        MU = w2flat[:, 512:1024]
        DI = w2flat[:, 1024:1536].bitcast(I32)
        VA = LO[:, 0:P]
        VB = LO[:, P:2 * P]
        vecA = sb("vecA", [P, 104])
        vecB = sb("vecB", [P, 104])
        cact = sb("cact", [P, KC])
        MOD = sb("MOD", [P, NADA, 24])
        GB = sb("GB", [P, D])
        DG = TG[:, :, :].rearrange("p a (b c) -> p (a b) c", c=P)
        ss = sb("ss", [P, NB])
        ms = sb("ms", [P, NB])
        rstd = sb("rstd", [P, NB])
        mhalf = sb("mhalf", [P, 8])
        mx = sb("mx", [P, 3])
        den = sb("den", [P, 2, NHA])
        rden = sb("rden", [P, 2, NHA])
        tmp = sb("tmp", [P, 2, 512])
        RWt = sb("RWt", [P, KC, NEXP])
        rb = sb("rb", [P, NEXP])
        ltm = sb("ltm", [P, 4, 4])
        tid = sb("tid", [P, NB])
        io128 = sb("io128", [P, P])
        W12 = sb("W12", [P, 2, NB])
        SLI = sb("SLI", [P, 2, NB], I32)
        CN = sb("CN", [1, 32], I32)
        LI = sb("LI", [P, 32], I32)
        IDX = sb("IDX", [P, 1], I32)
        bsT = vecB[:, 96:104]

        Xg = arena[:, 3, 0:1024]
        XgT = arena[:, 3, 1024:2048].rearrange("p (c t) -> p c t", c=KC)
        Yt = arena[:, 3, 2048:3072]
        sil = arena[:, 3, 3072:3328]
        hid = arena[:, 3, 3328:3584]
        hidT = arena[:, 3, 3584:3840].rearrange("p (c t) -> p c t", c=2)
        CB = arena[:, 6:8, :].rearrange("p a n -> p (a n)").rearrange("p (k f) -> p k f", k=8)

        xn_dram = nc.dram_tensor("xn_rows", (S, D), F32, kind="Internal").ap()
        y_dram = nc.dram_tensor("expert_rows", (MAX_ITEMS * P, D), F32, kind="Internal").ap()

        PS = ctx.enter_context(nc.psum_tensor("PS", [P, 8, 512], F32))

        SG = LO[:, 0:64]
        CHX = sb("CHX", [P, (NB + 1) * NEXP])
        CH = CHX[:, 0:NB * NEXP].rearrange("p (b e) -> p b e", b=NB)
        HOTI = LO[:, 896:1096].rearrange("p (k i) -> p k i", k=8)
        HOTR = LO[:, 1280:2304].rearrange("p (k r) -> p k r", k=8)
        SLF = sb("SLF", [P, 8])
        RI = sb("RI", [P, 2, 8], I32)
        RF = sb("RF", [P, 2, 8])

        def masks(v, link):
            ts, stt = nc.vector.tensor_scalar, nc.vector.scalar_tensor_tensor
            low = tmp[:, 0, :].bitcast(I32)
            v.wait_ge(sem("dist"), 1)
            link(ts(low, DI[:, :], 3, None, ALU.bitwise_and))
            link(ts(MU[:, :], low, 0.0, None, ALU.is_equal))
            link(ts(low, DI[:, :], 15, None, ALU.bitwise_and))
            link(stt(MU[:, :], low, 0.0, MU[:, :], ALU.is_equal, ALU.add))
            link(stt(MU[:, :], DI[:, :], float(SPAN), MU[:, :], ALU.is_le, ALU.add))
            link(stt(MU[:, :], DI[:, :], 0.0, MU[:, :], ALU.is_ge, ALU.mult))
            link(ts(MA[:, :], MU[:, :], 0.0, NEG, ALU.is_equal, ALU.mult))

        def route(v, link, layer, M):
            tt, ts, stt, red = (nc.vector.tensor_tensor, nc.vector.tensor_scalar, nc.vector.scalar_tensor_tensor,
                                nc.vector.tensor_reduce)
            G = NB * NGRP
            sel = LO[:, 64:128]
            A, B = LO[:, 128:384], LO[:, 384:640]
            rank, m1, m2 = LO[:, 640:704], LO[:, 704:768], LO[:, 768:832]
            at = [1096]

            def small(n):
                at[0] += n
                return LO[:, at[0] - n:at[0]]

            v1, v2, gs, grank, gsel = (small(G) for _ in range(5))
            s1, s2, su = (small(NB) for _ in range(3))
            nb, end, base = (small(NEXP) for _ in range(3))
            e3 = lambda a: a.rearrange("p (g j) -> p g j", j=EPG)
            b3 = lambda a: a.rearrange("p (b e) -> p b e", b=NB)

            def ranks(out, src, n):
                a4 = A[:, 0:16 * n].rearrange("p (g j i) -> p g j i", j=4, i=4)
                b4 = B[:, 0:16 * n].rearrange("p (g j i) -> p g j i", j=4, i=4)
                other = e3(src).unsqueeze(2).to_broadcast([P, n, 4, 4])
                own = e3(src).unsqueeze(3).to_broadcast([P, n, 4, 4])
                link(tt(a4, other, own, ALU.is_gt))
                link(tt(b4, other, own, ALU.is_equal))
                low = ltm[:, :, :].rearrange("p j i -> p (j i)").unsqueeze(1).to_broadcast([P, n, 16])
                link(tt(B[:, 0:16 * n].rearrange("p (g k) -> p g k", k=16),
                        B[:, 0:16 * n].rearrange("p (g k) -> p g k", k=16), low, ALU.mult))
                link(tt(A[:, 0:16 * n], A[:, 0:16 * n], B[:, 0:16 * n], ALU.add))
                link(red(out, A[:, 0:16 * n].rearrange("p (m i) -> p m i", i=4), AX, ALU.add))

            v.wait_ge(*free("logit", layer + 1))
            v.wait_ge(sem("rb_in"), 16)
            v.wait_ge(sem("moe_consts"), 5)
            link(tt(b3(sel), b3(SG), rb[:, :].unsqueeze(1).to_broadcast([P, NB, NEXP]), ALU.add))
            ranks(rank, sel, G)
            ts(m1, rank, 0.0, None, ALU.is_equal)
            link(ts(m2, rank, 1.0, None, ALU.is_equal))
            tt(A[:, 0:64], sel, m1, ALU.mult)
            link(tt(B[:, 0:64], sel, m2, ALU.mult))
            red(v1, e3(A[:, 0:64]), AX, ALU.add)
            link(red(v2, e3(B[:, 0:64]), AX, ALU.add))
            link(tt(gs, v1, v2, ALU.add))
            ranks(grank, gs, NB)
            link(ts(gsel, grank, 0.0, None, ALU.is_equal))
            gb = gsel.unsqueeze(2).to_broadcast([P, G, EPG])
            tt(e3(m1), e3(m1), gb, ALU.mult)
            link(tt(e3(m2), e3(m2), gb, ALU.mult))
            link(tt(CH.rearrange("p b e -> p (b e)"), m1, m2, ALU.add))
            tt(A[:, 0:64], SG, m1, ALU.mult).then_inc(M("chosen"), 1)
            link(tt(B[:, 0:64], SG, m2, ALU.mult))
            red(s1, b3(A[:, 0:64]), AX, ALU.add)
            link(red(s2, b3(B[:, 0:64]), AX, ALU.add))
            link(tt(su, s1, s2, ALU.add))
            link(nc.vector.reciprocal(su, su))
            tt(W12[:, 0, :], s1, su, ALU.mult)
            link(tt(W12[:, 1, :], s2, su, ALU.mult))
            v.wait_ge(*full("rank", layer + 1))
            ps = bank("rank", layer)
            tot = ps[:, 64:64 + NEXP]
            link(ts(nb, tot, 0.0, None, ALU.is_gt))
            for k in range(1, NB):
                link(stt(nb, tot, float(k * P), nb, ALU.is_gt, ALU.add))
            link(nc.vector.tensor_tensor_scan(end, ones[:, 0:NEXP], nb, 0.0, ALU.mult, ALU.add))
            link(tt(base, end, nb, ALU.subtract))
            link(ts(base, base, float(P), None, ALU.mult))
            tt(b3(rank), b3(ps[:, 0:64]), base.unsqueeze(1).to_broadcast([P, NB, NEXP]), ALU.add
               ).then_inc(drained["rank"], 1)
            v.wait_ge(*free("rank", layer + 1))
            tt(A[:, 0:64], rank, m1, ALU.mult)
            link(tt(B[:, 0:64], rank, m2, ALU.mult))
            red(SLF[:, 0:4], b3(A[:, 0:64]), AX, ALU.add)
            link(red(SLF[:, 4:8], b3(B[:, 0:64]), AX, ALU.add))
            sl = SLI[:, :, :].rearrange("p j b -> p (j b)")
            link(nc.vector.tensor_copy(sl, SLF[:, :]))
            ts(RI[:, 0, :], sl, P - 1, None, ALU.bitwise_and)
            link(ts(RI[:, 1, :], sl, 7, None, ALU.logical_shift_right))
            link(nc.vector.tensor_copy(RF[:, :, :], RI[:, :, :]))
            tt(HOTR, io128[:, :].unsqueeze(1).to_broadcast([P, 8, P]), RF[:, 0, :].unsqueeze(2).to_broadcast([P, 8, P]),
               ALU.is_equal)
            link(tt(HOTI, io128[:, 0:25].unsqueeze(1).to_broadcast([P, 8, 25]),
                    RF[:, 1, :].unsqueeze(2).to_broadcast([P, 8, 25]), ALU.is_equal))
            hot4 = HOTI.rearrange("p (j b) i -> p j b i", j=2)
            for j in range(2):
                last = tt(hot4[:, j], hot4[:, j], tid[:, :].unsqueeze(2).to_broadcast([P, NB, 25]), ALU.mult)
            last.then_inc(M("hot"), 1)
            it = LO[0:1, 128:512].rearrange("p (i e) -> p i e", e=NEXP)
            link(tt(it, end[0:1].unsqueeze(1).to_broadcast([1, MAX_ITEMS, NEXP]),
                    io128[0:1, 0:MAX_ITEMS].unsqueeze(2).to_broadcast([1, MAX_ITEMS, NEXP]), ALU.is_le))
            link(red(LO[0:1, 640:664], it, AX, ALU.add))
            nc.vector.tensor_copy(CN[0:1, 1:1 + MAX_ITEMS], LO[0:1, 640:664])
            nc.vector.tensor_copy(CN[0:1, 0:1], end[0:1, NEXP - 1:NEXP])
            v.wait_ge(*full("list", layer + 1))
            nc.vector.tensor_copy(LI[:, 0:25], bank("list", layer)[:, 0:25]).then_inc(drained["list"], 1)
            v.wait_ge(*free("list", layer + 1))
            nc.vector.engine_nop().then_inc(M("items"), 1)

        XX = area(2, "p (c t) -> p c t", c=KC)
        XM = [area(3, "p (c t) -> p c t", c=KC), area(4, "p (c t) -> p c t", c=KC)]
        V1 = area(5, "p (b f) -> p b f", b=NB)
        R1 = area(6, "p (c t) -> p c t", c=KC)
        K1 = area(7, "p (c t) -> p c t", c=KC)
        SGW, AA, KK = XM[0], XM[1], XX
        AR = HT
        RN = [GB[:, 0:512], GB[:, 512:1024]]
        W1L = LO[:, 0:512].rearrange("p (c f) -> p c f", c=KC)
        A1L = LO[:, 512:1024].rearrange("p (c f) -> p c f", c=KC)
        G1L = LO[:, 1024:2304].rearrange("p (c f) -> p c f", c=KC)
        WA2 = w2flat[:, 0:1024]
        BZ = w2flat[:, 1024:3072].rearrange("p (h m t) -> p h m t", h=2, m=2)
        G2A = arena[:, 4, 0:1024]
        G2B = arena[0:32, 4, 1024:2048]
        LNW = w2flat[:, 0:1024]
        LNB = TWA2[:, :]
        MK = w2flat[:, 3072:3584].bitcast(I32)
        t1 = arena[:, 1, :].rearrange("p (n j t) -> p n j t", n=8, j=NB)
        Tn = [t1[:, h] for h in range(2)]
        XT = [t1[:, 2 + h] for h in range(2)]
        Tt = [[t1[:, 4 + 2 * par + h] for h in range(2)] for par in range(2)]
        LT = [GB[:, h * 512:h * 512 + 512].rearrange("p (j t) -> p j t", j=NB) for h in range(2)]
        LM = [LO[:, h * 512:h * 512 + 512].rearrange("p (j t) -> p j t", j=NB) for h in range(2)]
        CU = LO[:, 1024:1536]
        E1 = LO[:, 1536:2048]
        wrf = WR[:, :, :, :].rearrange("p a b c -> p (a b c)")
        PM = [[wrf[:, (2 * par + h) * 1536:(2 * par + h + 1) * 1536].rearrange("p (j m t) -> p j m t", j=NB, m=3)
               for h in range(2)] for par in range(2)]
        BK = [wrf[:, 6144 + par * 1024:6144 + (par + 1) * 1024].rearrange("p (j m f) -> p j m f", j=NB, m=2)
              for par in range(2)]
        LV = sb("LV", [P, P])
        pairs = tmp[:, 1, 256:384].bitcast(I32)
        joins = tmp[:, 1, 384:512]
        NM = w2flat[:, 3584:4096]
        MID = sb("MID", [P, NB])
        EM = sb("EM", [P, NB])
        EE = sb("EE", [P, NB])
        DD = sb("DD", [P, 3, NB])
        BON = tmp[:, 1, 192:256].rearrange("p (c n) -> p c n", c=KC)
        RH = LO[:, 2048:2176].rearrange("p (h d) -> p h d", h=2)
        UU = LO[:, 2176:2304].rearrange("p (h d) -> p h d", h=2)
        ST = tmp[:, 1, 0:128].rearrange("p (h d) -> p h d", h=2)
        SD = tmp[:, 1, 128:192]
        oka = sb("oka", [P, KC])
        sm = sb("sm", [P, 4, 8])

        plan = bank_plan()
        drained_at = {}
        places = {"a": list(range(RING)), "b": list(range(RING, RING + LONG))}
        taken, seen = {}, {"a": 0, "b": 0}
        for kind, n, ring in plan:
            b = places[ring][seen[ring] % len(places[ring])]
            seen[ring] += 1
            drained_at[kind, n] = (b, taken.get(b))
            taken[b] = (kind, n)
        filled, full = shared(plan, FILLED_TOGETHER, "filled", sem)
        drained, free = shared(plan, EMPTIED_TOGETHER, "drained", sem)

        def bank(kind, n):
            return PS[:, drained_at[kind, n][0], :]

        def open_bank(pe, kind, n):
            b, before = drained_at[kind, n]
            if before:
                pe.wait_ge(*free(before[0], before[1] + 1))
            return PS[:, b, :]

        block = ctx.enter_context(nc.Block())

        tiles = [(io["mix_w_in"][0], n * 512) for n in range(5)] + [(io["mix_w_out"][0], n * 512) for n in range(2)]
        tile_last = [("q", 3), ("k", 3), ("v", 3), ("u", 3), ("z", 3), ("y", 3), ("y", 7)]
        for n, kind in ((2, "v1"), (0, "r1"), (1, "k1")):
            for half in range(2):
                tiles.append((io["rwkv_w_rkv"][0, n], half * 512))
                tile_last.append((kind, 4 * half + 3))
        for half in range(2):
            tiles.append((io["rwkv_w_o"][0], half * 512))
            tile_last.append(("y", 8 + 4 * half + 3))

        def tile_ready(eng, n):
            eng.wait_ge(sem(f"tile_in{n % 2}"), 16 * (n // 2 + 1))

        def moe_sem(layer, name):
            return sem(f"m{layer}_{name}")

        @block.sync
        def _(sp):
            sp.dma_start(VA[96:104, :], io["c"].rearrange("a (r p) -> (a r) p", p=P)).then_inc(sem("vec_in"), 16)
            sp.dma_start(VA[0:96, :], io["ada_b"].rearrange("l m (r p) -> (l m r) p", p=P)).then_inc(sem("vec_in"), 16)
            for r, name in ((0, "rwkv_mu"), (48, "rwkv_w0"), (56, "rwkv_a0"), (64, "rwkv_k_k"), (72, "rwkv_k_a"),
                            (80, "rwkv_r_k"), (96, "sgu_b")):
                v = io[name]
                if name == "rwkv_mu":
                    v = v.rearrange("l m (r p) -> (l m r) p", p=P)
                elif name == "rwkv_r_k":
                    v = v.rearrange("l (r two) d -> (l r) (two d)", two=2)
                elif name == "sgu_b":
                    v = v[0]
                else:
                    v = v.rearrange("l (r p) -> (l r) p", p=P)
                sp.dma_start(VB[r:r + v.shape[0], :], v).then_inc(sem("vec_in"), 16)
            sp.dma_start(VB[88:96, :], io["rwkv_w0"].rearrange("l (r p) -> (l r) p", p=P)).then_inc(sem("vec_in"), 16)

            def ada(L, m):
                n = L * 3 * KC + m
                if n >= 4:
                    sp.wait_ge(sem("ada_step"), n - 3)
                sp.dma_start(aring[:, n % 4, :],
                             io["ada_w"][L // 2, L % 2, (m % KC) * P:(m % KC + 1) * P,
                                         (m // KC) * D:(m // KC + 1) * D]
                             ).then_inc(sem(f"ada_in{n % 4}"), 16)

            def tile(n):
                if n >= 2:
                    k, at = tile_last[n - 2]
                    sp.wait_ge(*full(k, at + 1))
                w, col = tiles[n]
                sp.dma_start(WR[:, n % 2, :, :], w[:, col:col + 512].rearrange("(c p) f -> p c f", p=P)
                             ).then_inc(sem(f"tile_in{n % 2}"), 16)

            for m in range(4):
                ada(0, m)
            sp.dma_start(X, io["x"][0].rearrange("(b p) f -> p b f", p=P)).then_inc(sem("x_in"), 16)
            for m in range(4, 2 * KC):
                ada(0, m)
            tile(0)
            tile(1)
            for m in range(2 * KC, 3 * KC):
                ada(0, m)
            sp.dma_start(SW, io["sgu_w"][0].rearrange("g i j -> i g j")).then_inc(sem("sw_in"), 16)
            sp.dma_start(gz, io["sgu_norm_g"][0].partition_broadcast(P)).then_inc(sem("gz_in"), 16)
            sp.dma_start(RWt[:, :, :], io["router_w"].rearrange("(c p) e -> p c e", p=P)).then_inc(sem("rw_in"), 16)
            sp.dma_start(rb[:, :], io["router_b"].partition_broadcast(P)).then_inc(sem("rb_in"), 16)
            for m in range(3 * KC):
                ada(1, m)
                if m % 8 == 3:
                    tile(2 + m // 8)
            tile(5)
            tile(6)
            for L in (2, 3):
                for m in range(3 * KC):
                    ada(L, m)

            def moe(layer):
                M = lambda name: moe_sem(layer, name)
                sp.wait_ge(sem("xn"), NB * (2 * layer + 2))
                sp.dma_start(xn_dram.rearrange("(b p) f -> p b f", p=P), XN).then_inc(M("rows_out"), 16)
                sp.wait_ge(*full("y", 8 * (layer + 1)))
                sp.wait_ge(M("items"), 1)
                n = sp.value_load(CN[0:1, 0:1], min_val=8, max_val=MAX_ITEMS)

                def load(i, e, slot):
                    w = lambda name: io[name][layer][bass.ds(e, 1)]
                    sp.dma_start(WR[:, slot, :, 0:DEXP], w("moe_w1").rearrange("e (c p) f -> p (e c) f", p=P)
                                 ).then_inc(M("w1_in"), 16)
                    sp.dma_start(WR[:, slot, :, DEXP:2 * DEXP], w("moe_w3").rearrange("e (c p) f -> p (e c) f", p=P)
                                 ).then_inc(M("w3_in"), 16)
                    sp.dma_start(W2[:, slot, :, :], w("moe_w2").rearrange("e (c p) f -> p (e c) f", p=P)
                                 ).then_inc(M("w2_in"), 16)

                def earlier(count):
                    sp.wait_ge(M("w1_in"), count)
                    sp.wait_ge(M("w3_in"), count)
                    sp.wait_ge(M("w2_in"), count)

                for i in range(2):
                    e = sp.value_load(CN[0:1, i + 1:i + 2], min_val=0, max_val=NEXP - 1)
                    if i:
                        earlier(i * 16)
                    load(i, e, i)
                if layer == 0:
                    sp.dma_start(W1L, io["rwkv_w1"][0].rearrange("(c p) f -> p c f", p=P)).then_inc(sem("lora_in"), 16)
                    sp.dma_start(A1L, io["rwkv_a1"][0].rearrange("(c p) f -> p c f", p=P)).then_inc(sem("lora_in"), 16)
                    sp.dma_start(G1L, io["rwkv_g1"][0].rearrange("(c p) f -> p c f", p=P)).then_inc(sem("lora_in"), 16)
                used, loaded = sp.alloc_register(f"used{layer}"), sp.alloc_register(f"loaded{layer}")
                sp.reg_mov(used, 1)
                sp.reg_mov(loaded, 32)
                with sp.Fori(2, n) as i:
                    e = sp.value_load(CN[0:1, bass.ds(i + 1, 1)], min_val=0, max_val=NEXP - 1)
                    sp.wait_ge(M("items"), 1)
                    sp.wait_ge(M("up"), used)
                    sp.wait_ge(M("down"), used)
                    earlier(loaded)
                    w = lambda name: io[name][layer][bass.ds(e, 1)]
                    slot = bass.ds(i % 2, 1)
                    sp.dma_start(WR[:, slot, :, 0:DEXP].rearrange("p s c f -> p (s c) f"),
                                 w("moe_w1").rearrange("e (c p) f -> p (e c) f", p=P)).then_inc(M("w1_in"), 16)
                    sp.dma_start(WR[:, slot, :, DEXP:2 * DEXP].rearrange("p s c f -> p (s c) f"),
                                 w("moe_w3").rearrange("e (c p) f -> p (e c) f", p=P)).then_inc(M("w3_in"), 16)
                    sp.dma_start(W2[:, slot, :, :].rearrange("p s c f -> p (s c) f"),
                                 w("moe_w2").rearrange("e (c p) f -> p (e c) f", p=P)).then_inc(M("w2_in"), 16)
                    sp.reg_add(used, used, 1)
                    sp.reg_add(loaded, loaded, 16)

            moe(0)
            n = sp.value_load(CN[0:1, 0:1], min_val=8, max_val=MAX_ITEMS)
            sp.wait_ge(moe_sem(0, "items"), 1)
            sp.wait_ge(moe_sem(0, "down"), n)
            for k in range(3):
                sp.wait_ge(moe_sem(0, f"w{k + 1}_in"), n * 16)
            sp.wait_ge(moe_sem(0, f"pair_in{NB - 1}"), 32)
            tile(7)
            tile(8)
            sp.dma_start(WA2[0:HD, :], io["rwkv_w2"][0]).then_inc(sem("wa2_in"), 16)
            sp.dma_start(WA2[HD:P, :], io["rwkv_a2"][0]).then_inc(sem("wa2_in"), 16)
            for n in range(9, 13):
                tile(n)
            sp.wait_ge(*full("za", KC))
            sp.dma_start(LNW, io["rwkv_ln_w"][0].partition_broadcast(P)).then_inc(sem("ln_in"), 16)
            sp.dma_start(LNB, io["rwkv_ln_b"][0].partition_broadcast(P)).then_inc(sem("ln_in"), 16)
            sp.wait_ge(sem("prep_done"), 4)
            sp.dma_start(G2A, io["rwkv_g2"][0, 0:P, :]).then_inc(sem("g2_in"), 16)
            sp.dma_start(G2B, io["rwkv_g2"][0, P:P + 32, :]).then_inc(sem("g2_in"), 16)
            sp.wait_ge(*full("Y", 8 * KC))
            tile(13)
            tile(14)
            moe(1)
            sp.wait_ge(sem("x_done"), 25)
            sp.dma_start(LNW, io["final_norm_g"].partition_broadcast(P)).then_inc(sem("fin_in"), 16)
            for b in range(NB):
                sp.wait_ge(sem("fin"), b + 1)
                sp.dma_start(io["out"][0, b * P:(b + 1) * P, :], XN[:, b, :]).then_inc(sem("out_done"), 16)
            sp.wait_ge(sem("out_done"), 16 * NB)

        @block.gpsimd
        def _(gp):
            done = [0]

            def link(ins):
                done[0] += 1
                ins.then_inc(sem("pool_chain"), 1)
                gp.wait_ge(sem("pool_chain"), done[0])

            link(gp.memset(ident[:, :], 0.0))
            gp.affine_select(out=ident[:, :], in_=ident[:, :], compare_op=ALU.not_equal, fill=1.0, base=0,
                             pattern=[[-1, P]], channel_multiplier=1).then_inc(sem("ident_ready"), 1)
            gp.memset(ones[:, :], 1.0).then_inc(sem("ones_ready"), 1)
            gp.memset(mhalf[:, :], -0.5).then_inc(sem("mhalf_ready"), 1)
            gp.iota(DI[:, :], pattern=[[-1, S]], base=S - P, channel_multiplier=1).then_inc(sem("dist"), 1)
            gp.iota(io128[:, :], pattern=[[1, P]], base=0, channel_multiplier=0,
                    allow_small_or_imprecise_dtypes=True).then_inc(sem("moe_consts"), 1)
            gp.iota(tid[:, :], pattern=[[P, NB]], base=0, channel_multiplier=1,
                    allow_small_or_imprecise_dtypes=True).then_inc(sem("moe_consts"), 1)
            link(gp.memset(ltm[:, :, :], 1.0))
            gp.affine_select(out=ltm[:, :, :], in_=ltm[:, :, :], compare_op=ALU.is_gt, fill=0.0, base=0,
                             pattern=[[1, 4], [-1, 4]], channel_multiplier=0).then_inc(sem("moe_consts"), 1)
            gp.memset(CHX[:, :], 0.0).then_inc(sem("moe_consts"), 1)
            link(gp.memset(upper[:, :], 1.0))
            gp.affine_select(out=upper[:, :], in_=upper[:, :], compare_op=ALU.is_gt, fill=0.0, base=0,
                             pattern=[[1, P]], channel_multiplier=-1).then_inc(sem("moe_consts"), 1)
            def level(gp, c, h, lv):
                n = 2 * (LEVELS - 1) * c + 2 * lv + h
                if c or lv:
                    gp.wait_ge(*full("X", 2 * LEVELS * c + 2 * lv + h - 1 - (2 if lv == 0 else 0)))
                if h == 0:
                    if n:
                        gp.wait_ge(sem("lm_ready"), n)
                    link(gp.tensor_scalar(joins[:, :], LV[:, :], float(lv + 2), None, ALU.is_equal))
                gp.tensor_tensor(LM[h], LT[h], joins[:, :].unsqueeze(1).to_broadcast([P, NB, P]), ALU.mult
                                 ).then_inc(sem("lm_ready"), 1)

            def rms(n):
                gp.wait_ge(sem("ms_ready"), n + 1)
                gp.tensor_tensor(rstd[:, :], ms[:, :], mhalf[:, 0:NB], ALU.pow).then_inc(sem("rstd_ready"), 1)

            gp.wait_ge(sem("mhalf_ready"), 1)
            rms(0)
            gp.wait_ge(sem("sw_in"), 16)
            gp.affine_select(out=SW, in_=SW, compare_op=ALU.is_ge, fill=0.0, base=0,
                             pattern=[[0, NHA], [-1, P]], channel_multiplier=1).then_inc(sem("swm"), 1)
            rms(1)

            def moe(layer):
                M = lambda name: moe_sem(layer, name)
                rms(2 + 2 * layer)
                gp.wait_ge(M("items"), 1)
                gp.wait_ge(M("rows_out"), 16)
                n = gp.value_load(CN[0:1, 0:1], min_val=8, max_val=MAX_ITEMS)
                src = bass.IndirectOffsetOnAxis(ap=IDX[:, 0:1], axis=0)
                gp.tensor_copy(IDX[:, :], LI[:, 0:1]).then_inc(M("idx"), 1)
                gp.wait_ge(M("idx"), 1)
                gp.indirect_dma_start(Xg, None, xn_dram, src).then_inc(M("xg_in"), 16)
                indexed, turned = gp.alloc_register(f"indexed{layer}"), gp.alloc_register(f"turned{layer}")
                gathered = gp.alloc_register(f"gathered{layer}")
                gp.reg_mov(gathered, 0)
                if layer == 0:
                    rest = gp.alloc_register("rest")
                    gp.reg_mov(rest, 0)
                    with gp.Fori(n, MAX_ITEMS):
                        gp.reg_add(rest, rest, 16)
                gp.reg_mov(indexed, 2)
                gp.reg_mov(turned, 1)
                with gp.Fori(0, n) as i:
                    gp.wait_ge(M("xg_in"), i * 16 + 16)
                    gp.tensor_copy(IDX[:, :], LI[:, bass.ds(i + 1, 1)]).then_inc(M("idx"), 1)
                    gp.wait_ge(M("rows_out"), 16)
                    gp.wait_ge(M("idx"), indexed)
                    gp.wait_ge(M("tx"), turned)
                    gp.reg_add(indexed, indexed, 1)
                    gp.reg_add(turned, turned, 1)
                    gp.reg_add(gathered, gathered, 16)
                    gp.indirect_dma_start(Xg, None, xn_dram, src).then_inc(M("xg_in"), 16)
                if layer == 0:
                    gp.wait_ge(sem("rest_out"), rest)
                gp.wait_ge(M("row_out"), n * 16 + 16)
                gp.reg_add(gathered, gathered, 16)
                gp.wait_ge(M("rows_out"), 16)
                gp.wait_ge(M("xg_in"), gathered)
                for b in range(NB):
                    for j in range(2):
                        gp.indirect_dma_start(CB[:, 2 * b + j, :], None, y_dram,
                                              bass.IndirectOffsetOnAxis(ap=SLI[:, j, b:b + 1], axis=0)
                                              ).then_inc(M(f"pair_in{b}"), 16)

            moe(0)
            rms(3)
            link(gp.memset(blk[:, :], 0.0))
            link(gp.memset(blk[0:HD, 0:HD], 1.0))
            gp.memset(blk[HD:P, HD:P], 1.0).then_inc(sem("blk_ready"), 1)
            gp.wait_ge(sem("blk_ready"), 1)
            link(gp.memset(NM[:, :], 1.0))
            gp.memset(BZ[:, :, :, :], 0.0).then_inc(sem("zeroed"), 1)
            gp.memset(NM[:, 0:S:P], 0.0).then_inc(sem("blk_ready"), 1)
            gp.wait_ge(sem("levels"), 1)
            gp.wait_ge(*full("k1", 8))
            gp.wait_ge(sem("knorm"), KC)
            gp.memset(wrf[:, 0:6144], 0.0).then_inc(sem("zeroed"), 1)
            gp.wait_ge(sem("kk_unit"), KC)
            gp.memset(GB[:, :], 0.0).then_inc(sem("zeroed"), 1)
            gp.wait_ge(sem("added_key"), 1)
            for c in range(1, KC):
                gp.tensor_tensor(AA[:, c, :], AR[:, c, :], KK[:, c, :], ALU.mult).then_inc(sem("added_key"), 1)
            gp.wait_ge(sem("added_key"), KC)
            for step in scan_steps():
                if step[0] == "turn":
                    c = step[1]
                    if c >= 2:
                        gp.wait_ge(*full("U", 8 * (c - 1)))
                    for h in range(2):
                        gp.tensor_copy(Tt[c % 2][h], ident[:, :].unsqueeze(1).to_broadcast([P, NB, P])
                                       ).then_inc(sem("unit"), 1)
                elif step[0] == "lower":
                    _, c, h = step
                    gp.wait_ge(sem("lt_ready"), NB * (2 * c + h + 1))
                    level(gp, c, h, 0)
                elif step[0] == "T" and step[3] < LEVELS - 2:
                    level(gp, step[1], step[2], step[3] + 1)
                elif step[0] == "rstd":
                    c = step[1]
                    gp.wait_ge(sem("gn_var"), c + 1)
                    gp.tensor_tensor(sm[:, 3, :], sm[:, 2, :], mhalf[:, 0:8], ALU.pow).then_inc(sem("gn_rstd"), 1)
                elif step[0] == "output":
                    c = step[1]
                    y3 = SGW[:, c, :].rearrange("p (j f) -> p j f", j=NB)
                    if c == 0:
                        gp.wait_ge(sem("ln_in"), 32)
                    bc = lambda a: a[:, c * P:(c + 1) * P].unsqueeze(1).to_broadcast([P, NB, P])
                    gp.wait_ge(sem("gn_y"), c + 1)
                    link(gp.tensor_tensor(y3, y3, bc(LNW), ALU.mult))
                    link(gp.tensor_tensor(y3, y3, bc(LNB), ALU.add))
                    v3 = V1[:, :, c * P:(c + 1) * P]
                    gp.wait_ge(sem("gn_bv"), c + 1)
                    gp.tensor_tensor(v3, v3, y3, ALU.add).then_inc(sem("y_ready"), 1)
            moe(1)
            rms(5)

        @block.scalar
        def _(act):
            def squares(n):
                if n == 0:
                    act.wait_ge(sem("x_in"), 16)
                for b in range(NB):
                    if n % 2:
                        act.wait_ge(sem("x_done"), 8 * (n - 1) + NB + b + 1)
                    elif n:
                        act.wait_ge(sem("x_done"), 8 * (n - 1) + 2 * b + 2)
                    nc.scalar.activation(XN[:, b, :], X[:, b, :], ACT.Square, accum_out=ss[:, b:b + 1]
                                         ).then_inc(sem("ss_ready"), 1)

            def hT(n, L):
                for c in range(1, KC, 2):
                    k = 4 * n + c // 2
                    act.wait_ge(*full("xTa", k + 1))
                    if c == 1:
                        act.wait_ge(sem("mod_ready"), L + 2)
                    nc.scalar.activation(HT[:, c, :], bank("xTa", k), ACT.Identity, bias=MOD[:, L, c:c + 1],
                                         scale=MOD[:, L, 8 + c:9 + c]).then_inc(drained["xTa"], 1)

            def gate(k):
                if k:
                    act.wait_ge(sem("x_done"), 8 * k)
                for half in range(2):
                    act.wait_ge(*full("gate", 2 * k + half + 1))
                    nc.scalar.copy(GB[:, half * 512:half * 512 + 512], bank("gate", 2 * k + half)
                                   ).then_inc(drained["gate"], 1)

            act.wait_ge(*free("vec", 1))
            nc.scalar.activation(cact[:, :], vecA[:, 96:104], ACT.Silu).then_inc(sem("c_ready"), 1)
            squares(0)
            for c in range(1, KC, 2):
                act.wait_ge(*full("xTa", c // 2 + 1))
                nc.scalar.copy(HT[:, c, :], bank("xTa", c // 2)).then_inc(drained["xTa"], 1)
            act.wait_ge(sem("mod_ready"), 1)
            act.wait_ge(*free("xTa", 4))
            for c in range(1, KC, 2):
                nc.scalar.activation(HT[:, c, :], HT[:, c, :], ACT.Identity, bias=MOD[:, 0, c:c + 1],
                                     scale=MOD[:, 0, 8 + c:9 + c]).then_inc(sem("h0_ready"), 1)
            for f in range(4):
                act.wait_ge(*full("k", f + 1))
                nc.scalar.copy(kT[:, f, :], bank("k", f)).then_inc(drained["k"], 1)
            for b in range(NB):
                act.wait_ge(*full("u", b + 1))
                nc.scalar.activation(U0[:, b, :], bank("u", b), ACT.Gelu).then_inc(drained["u"], 1)
            for b in range(NB):
                act.wait_ge(*full("z", b + 1))
                nc.scalar.activation(Z0[:, b, :], bank("z", b), ACT.Gelu).then_inc(drained["z"], 1)
                act.wait_ge(*free("z", b + 1))
                nc.scalar.activation(OB[:, 0, :], Z0[:, b, :], ACT.Square, accum_out=ss[:, b:b + 1]
                                     ).then_inc(sem("zss_ready"), 1)
            for n in range(NB * NHA + 3):
                if n < NB * NHA:
                    i = n // NHA
                    act.wait_ge(*free("score", n + 1))
                    row = Pb[:, n % 3, 0:(i + 1) * P]
                    nc.scalar.activation(row, row, ACT.Exp, bias=mx[:, n % 3:n % 3 + 1], scale=-1.0
                                         ).then_inc(sem("probs"), 1)
                if 2 <= n <= NB * NHA + 1:
                    m = n - 2
                    i = m // NHA
                    act.wait_ge(*full("pT", m + 1))
                    if m >= 3:
                        act.wait_ge(sem("pv"), m - 2)
                    nc.scalar.copy(PT[:, m % 3, 0:(i + 1) * P], bank("pT", m)[:, 0:(i + 1) * P]
                                   ).then_inc(drained["pT"], 1)
                if n >= 3 and (n - 3) % NHA == NHA - 1:
                    i = (n - 3) // NHA
                    act.wait_ge(*full("oT", i + 1))
                    nc.scalar.copy(HT[:, 0:4, i * P:(i + 1) * P], bank("oT", i).rearrange("p (c t) -> p c t", c=4)
                                   ).then_inc(drained["oT"], 1)
            for k in range(2):
                act.wait_ge(*full("swT", k + 1))
                nc.scalar.copy(SWT[:, 4 * k:4 * k + 4, :], bank("swT", k).rearrange("p (c t) -> p c t", c=4)
                               ).then_inc(drained["swT"], 1)
            for b in range(NB):
                act.wait_ge(*full("sT", b + 1))
                nc.scalar.copy(HT[:, 4:8, b * P:(b + 1) * P], bank("sT", b).rearrange("p (c t) -> p c t", c=4)
                               ).then_inc(drained["sT"], 1)
            gate(0)

            def moe(layer):
                M = lambda name: moe_sem(layer, name)
                L = 2 * layer + 1
                squares(L)
                hT(L, L)
                act.wait_ge(*full("logit", layer + 1))
                nc.scalar.activation(SG[:, :], bank("logit", layer)[:, 0:64], ACT.Sigmoid
                                     ).then_inc(drained["logit"], 1)
                gate(L)
                act.wait_ge(M("items"), 1)
                n = act.value_load(CN[0:1, 0:1], min_val=8, max_val=MAX_ITEMS)

                def turned(wait):
                    act.wait_ge(M("tx"), wait)
                    for c in range(4):
                        last = nc.scalar.activation(XgT[:, c, :], PS[:, 0, c * P:(c + 1) * P], ACT.Identity,
                                                    bias=MOD[:, L, c:c + 1], scale=MOD[:, L, 8 + c:9 + c])
                    last.then_inc(M("xga"), 1)

                if layer == 0:
                    act.wait_ge(sem("xn"), NB * 2)
                    with act.Fori(n, MAX_ITEMS) as k:
                        act.dma_start(y_dram[bass.ds(k * P, P), :], XN[:, 0, :]).then_inc(sem("rest_out"), 16)
                turned(1)
                with act.Fori(0, n) as i:
                    act.wait_ge(M("up"), i + 1)
                    act.wait_ge(M("hid"), i + 1)
                    nc.scalar.activation(sil, PS[:, 2, 0:DEXP], ACT.Silu).then_inc(M("sil"), 1)
                    turned(i + 2)
                    act.wait_ge(M("yt"), i + 2)
                    act.dma_start(y_dram[bass.ds(i * P, P), :], Yt).then_inc(M("row_out"), 16)

            moe(0)

            def copy(dst, kind, k, src, func=ACT.Copy):
                act.wait_ge(*full(kind, k + 1))
                nc.scalar.activation(dst, src, func).then_inc(drained[kind], 1)

            def rwkv():
                squares(2)
                hT(2, 2)
                for k in range(8):
                    half, b = k // 4, k % 4
                    copy(V1[:, b, half * 512:half * 512 + 512], "v1", k, bank("v1", k))
                act.wait_ge(*full("wl", 1))
                nc.scalar.activation(TWA[0:HD, :], bank("wl", 0)[0:HD, :], ACT.Tanh).then_inc(drained["wl"], 1)
                copy(TWA[HD:P, :], "al", 0, bank("al", 0)[HD:P, :])
                copy(TG[:, 0, :], "gl", 0, bank("gl", 0), ACT.Sigmoid)
                copy(TG[0:32, 1, :], "gl", 1, bank("gl", 1)[0:32, :], ACT.Sigmoid)
                for c in range(KC):
                    copy(R1[:, c, :], "r1", c, bank("r1", c))

                def norm(c):
                    act.wait_ge(*free("nrm", c + 1))
                    nc.scalar.activation(RN[c % 2], RN[c % 2], ACT.Sqrt).then_inc(sem("knorm"), 1)

                for c in range(KC):
                    act.wait_ge(*full("zw", c + 1))
                    nc.scalar.activation(SGW[:, c, :], bank("zw", c), ACT.Sigmoid, bias=vecB[:, 48 + c:49 + c]
                                         ).then_inc(drained["zw"], 1)
                    act.wait_ge(*full("za", c + 1))
                    if c == 0:
                        act.wait_ge(sem("mixed"), 48)
                    nc.scalar.activation(AR[:, c, :], bank("za", c), ACT.Sigmoid, bias=vecB[:, 56 + c:57 + c]
                                         ).then_inc(drained["za"], 1)
                    act.wait_ge(sem("kkr"), c + 1)
                    if c >= 2:
                        act.wait_ge(*full("nrm", c - 1))
                    sq = (CU, E1)[c % 2]
                    nc.scalar.activation(sq, KK[:, c, :], ACT.Square).then_inc(sem("ksq"), 1)
                    if c:
                        norm(c - 1)
                norm(KC - 1)
                n_sc = {k: 0 for k in ("X", "N", "U", "Y")}
                for step in scan_steps():
                    kind = step[0]
                    if kind == "exponents":
                        c = step[1]
                        act.wait_ge(sem("cc"), c + 1)
                        nc.scalar.activation(E1, CU, ACT.Exp, scale=-KAPPA).then_inc(sem("e1"), 1)
                        nc.scalar.activation(EM[:, :], MID[:, :], ACT.Exp, scale=-KAPPA)
                        nc.scalar.activation(EE[:, :], CU[:, P - 1:S:P], ACT.Exp, scale=-KAPPA).then_inc(sem("ee"), 1)
                    elif kind == "exponents2":
                        c = step[1]
                        act.wait_ge(sem("ce"), c + 1)
                        nc.scalar.activation(SGW[:, c, :], SGW[:, c, :], ACT.Exp, scale=-KAPPA).then_inc(sem("e2"), 1)
                        act.wait_ge(sem("ee"), c + 1)
                        nc.scalar.activation(CU, CU, ACT.Exp, scale=KAPPA).then_inc(sem("e3"), 1)
                    elif kind == "turn":
                        c = step[1]
                        for h in range(2):
                            if c >= 2:
                                act.wait_ge(*full("dS", 6 * (c - 1)))
                            copy(BK[c % 2][:, :, :, h * HD:(h + 1) * HD].rearrange("p j m f -> p (j m) f"), "bkT",
                                 2 * c + h, bank("bkT", 2 * c + h).rearrange("p (q f) -> p q f", q=2 * NB))
                    elif kind == "lower":
                        _, c, h = step
                        copy(Tn[h], "lo", 2 * c + h, bank("lo", 2 * c + h).rearrange("p (j t) -> p j t", j=NB))
                    elif kind == "X":
                        _, c, h, lv = step
                        n = n_sc["X"]
                        n_sc["X"] += 1
                        if n >= 2:
                            act.wait_ge(*full("Tt", n - 1))
                        if lv < LEVELS - 1:
                            copy(XT[h], "X", n, bank("X", n).rearrange("p (j t) -> p j t", j=NB))
                        else:
                            copy(XT[h][HD:P, :, 0:HD], "X", n,
                                 bank("X", n)[HD:P, 0:NB * HD].rearrange("p (j t) -> p j t", j=NB))
                    elif kind == "N":
                        _, c, h, lv = step
                        n = n_sc["N"]
                        n_sc["N"] += 1
                        if lv < LEVELS - 2:
                            copy(Tn[h], "Tn", n, bank("Tn", n).rearrange("p (j t) -> p j t", j=NB))
                        else:
                            copy(Tn[h][0:HD, :, 0:HD], "Tn", n,
                                 bank("Tn", n)[0:HD, 0:NB * HD].rearrange("p (j t) -> p j t", j=NB))
                    elif kind == "U":
                        _, c, h, j = step
                        n = n_sc["U"]
                        n_sc["U"] += 1
                        if n >= 2:
                            act.wait_ge(*full("Y", n - 1))
                        if j and n >= 2:
                            act.wait_ge(*full("dS", 6 * c + 2 * (j - 1) + h + 1))
                        copy(UU[:, h, :], "U", n, bank("U", n)[:, 0:HD])
                    elif kind == "Y":
                        _, c, h, j = step
                        n = n_sc["Y"]
                        n_sc["Y"] += 1
                        act.wait_ge(sem("prep_done"), c + 1)
                        copy(SGW[:, c, j * P + h * HD:j * P + (h + 1) * HD], "Y", n, bank("Y", n)[:, 0:HD])
                    elif kind == "square":
                        c = step[1]
                        act.wait_ge(sem("gn_mean"), c + 1)
                        nc.scalar.activation(KK[:, c, :], SGW[:, c, :], ACT.Square).then_inc(sem("gn_sq"), 1)
                for c in range(KC):
                    copy(HT[:, c, :], "yT", c, bank("yT", c))
                gate(2)

            rwkv()
            moe(1)
            squares(4)

        @block.vector
        def _(v):
            done = [0]

            def link(ins):
                done[0] += 1
                ins.then_inc(sem("dve_chain"), 1)
                v.wait_ge(sem("dve_chain"), done[0])

            tt, ts, stt, red = (nc.vector.tensor_tensor, nc.vector.tensor_scalar, nc.vector.scalar_tensor_tensor,
                                nc.vector.tensor_reduce)

            def ada(L, m):
                n = L * 3 * KC + m
                c, third = m % KC, m // KC
                a = acc[:, third * D:(third + 1) * D]
                v.wait_ge(sem(f"ada_in{n % 4}"), 16 * (n // 4 + 1))
                if n == 0:
                    v.wait_ge(sem("c_ready"), 1)
                else:
                    v.wait_ge(sem("ada_step"), n)
                if c == 0:
                    if L:
                        v.wait_ge(*full("mod", L + 1))
                    ts(a, aring[:, n % 4, :], cact[:, 0:1], None, ALU.mult).then_inc(sem("ada_step"), 1)
                else:
                    stt(a, aring[:, n % 4, :], cact[:, c:c + 1], a, ALU.mult, ALU.add).then_inc(sem("ada_step"), 1)

            def mod(k):
                L, cols = (0, (slice(0, 16), slice(16, 24))[k]) if k < 2 else (k - 1, slice(0, 24))
                v.wait_ge(*full("mod", k + 1))
                tt(MOD[:, L, cols], bank("mod", k)[:, cols], vecA[:, 24 * L + cols.start:24 * L + cols.stop], ALU.add
                   ).then_inc(drained["mod"], 1)
                v.wait_ge(*free("mod", k + 1))
                if k != 1:
                    ts(MOD[:, L, 8:16], MOD[:, L, 8:16], 1.0, None, ALU.add).then_inc(sem("mod_ready"), 1)
                else:
                    nc.vector.engine_nop().then_inc(sem("mod_ready"), 1)

            def rms(n, sums, count, width):
                v.wait_ge(sums, count)
                ts(ms[:, :], ss[:, :], 1.0 / width, EPS, ALU.mult, ALU.add).then_inc(sem("ms_ready"), 1)
                v.wait_ge(sem("rstd_ready"), n + 1)

            def normed(n):
                for b in range(NB):
                    ts(XN[:, b, :], X[:, b, :], rstd[:, b:b + 1], None, ALU.mult).then_inc(sem("xn"), 1)

            def hT(n, L):
                for c in range(0, KC, 2):
                    k = 4 * n + c // 2
                    v.wait_ge(*full("xTv", k + 1))
                    if c == 0:
                        v.wait_ge(sem("mod_ready"), L + 2)
                    ts(HT[:, c, :], bank("xTv", k), MOD[:, L, 8 + c:9 + c], MOD[:, L, c:c + 1], ALU.mult, ALU.add
                       ).then_inc(drained["xTv"], 1)

            def diag(k, L):
                if k:
                    v.wait_ge(*full("gate", 2 * k))
                for c in range(KC):
                    ts(DG[:, c, :], ident[:, :], MOD[:, L, 16 + c:17 + c], None, ALU.mult
                       ).then_inc(sem("diag"), 1)

            def residual(layer):
                v.wait_ge(*free("gate", 2 * (2 * layer + 1)))
                for n in range(8):
                    half, b = n // 4, n % 4
                    k = 8 * layer + n
                    v.wait_ge(*full("y", k + 1))
                    cols = slice(half * 512, half * 512 + 512)
                    tt(tmp[:, n % 2, :], bank("y", k), GB[:, cols], ALU.mult).then_inc(drained["y"], 1)
                    v.wait_ge(*free("y", k + 1))
                    tt(X[:, b, cols], X[:, b, cols], tmp[:, n % 2, :], ALU.add).then_inc(sem("x_done"), 1)

            masks(v, link)
            for k, (dst, _) in enumerate(((vecA, VA), (vecB, VB))):
                v.wait_ge(*full("vec", k + 1))
                nc.vector.tensor_copy(dst[:, :], bank("vec", k)[:, 0:104]).then_inc(drained["vec"], 1)
            for m in range(13):
                ada(0, m)
            rms(0, sem("ss_ready"), 4, D)
            normed(0)
            for m in range(13, 14):
                ada(0, m)
            for c in range(0, KC, 2):
                v.wait_ge(*full("xTv", c // 2 + 1))
                nc.vector.tensor_copy(HT[:, c, :], bank("xTv", c // 2)).then_inc(drained["xTv"], 1)
            for m in range(14, 2 * KC):
                ada(0, m)
            mod(0)
            v.wait_ge(sem("mod_ready"), 1)
            v.wait_ge(*free("xTv", 4))
            for c in range(0, KC, 2):
                ts(HT[:, c, :], HT[:, c, :], MOD[:, 0, 8 + c:9 + c], MOD[:, 0, c:c + 1], ALU.mult, ALU.add
                   ).then_inc(sem("h0_ready"), 1)
            todo = [(0, m) for m in range(2 * KC, 3 * KC)] + [(L, m) for L in (1, 2, 3) for m in range(3 * KC)]

            def some_ada(n):
                for _ in range(n):
                    ada(*todo.pop(0))

            for f in range(4):
                v.wait_ge(*full("q", f + 1))
                ts(qT[:, f, :], bank("q", f), -(HD ** -0.5), None, ALU.mult).then_inc(drained["q"], 1)
                some_ada(2)
            mod(1)
            for f in range(4):
                some_ada(2)
                v.wait_ge(*full("k", f + 1))
            for b in range(NB):
                v.wait_ge(*full("v", b + 1))
                nc.vector.tensor_copy(V0[:, b, :], bank("v", b)).then_inc(drained["v"], 1)
                some_ada(2)
            for b in range(NB):
                some_ada(2)
            mod(2)
            rms(1, sem("zss_ready"), 4, WA)
            v.wait_ge(sem("gz_in"), 16)
            for b in range(NB):
                stt(Z0[:, b, :], Z0[:, b, :], rstd[:, b:b + 1], gz, ALU.mult, ALU.mult).then_inc(sem("zn"), 1)

            for n in range(NB * NHA + 3):
                if n < NB * NHA:
                    i = n // NHA
                    cols = slice((NB - 1 - i) * P, S)
                    v.wait_ge(*full("score", n + 1))
                    if n >= 3:
                        v.wait_ge(*full("pT", n - 2))
                        v.wait_ge(sem("probs"), n - 2)
                    nc.vector.tensor_tensor_reduce(Pb[:, n % 3, 0:(i + 1) * P], bank("score", n)[:, 0:(i + 1) * P],
                                                   MA[:, cols], 1.0, 3e38, ALU.add, ALU.min, mx[:, n % 3:n % 3 + 1]
                                                   ).then_inc(drained["score"], 1)
                if 1 <= n <= NB * NHA:
                    m = n - 1
                    i = m // NHA
                    cols = slice((NB - 1 - i) * P, S)
                    v.wait_ge(sem("probs"), m + 1)
                    row = Pb[:, m % 3, 0:(i + 1) * P]
                    nc.vector.tensor_tensor_reduce(row, row, MU[:, cols], 1.0, 0.0, ALU.mult, ALU.add,
                                                   den[:, i % 2, m % NHA:m % NHA + 1]).then_inc(sem("pm"), 1)
                if n >= 3 and (n - 3) % NHA == NHA - 1:
                    i = (n - 3) // NHA
                    v.wait_ge(sem("pm"), NHA * (i + 1))
                    link(nc.vector.reciprocal(rden[:, i % 2, :], den[:, i % 2, :]))
                    v.wait_ge(sem("pv"), NHA * (i + 1))
                    if i >= 2:
                        v.wait_ge(*full("oT", i - 1))
                    tt(OB[:, i % 2, :].rearrange("p (h d) -> p h d", h=NHA),
                       bank("o", i).rearrange("p (h d) -> p h d", h=NHA),
                       rden[:, i % 2, :].unsqueeze(2).to_broadcast([P, NHA, HD]), ALU.mult
                       ).then_inc(drained["o"], 1)
                if todo[0][0] == 2:
                    some_ada(1)
            for b in range(NB):
                v.wait_ge(*full("mix", b + 1))
                if b < 2:
                    v.wait_ge(*full("oT", 3 + b))
                else:
                    v.wait_ge(*full("sT", b - 1))
                g = lambda a: a.rearrange("p (h d) -> p h d", h=NHA)
                tt(g(OB[:, b % 2, :]), g(bank("mix", b)), bsT.unsqueeze(2).to_broadcast([P, NHA, HD]), ALU.add
                   ).then_inc(drained["mix"], 1)
                v.wait_ge(*free("mix", b + 1))
                v.wait_ge(*free("u", b + 1))
                tt(OB[:, b % 2, :], OB[:, b % 2, :], U0[:, b, :], ALU.mult).then_inc(sem("sgu_ob"), 1)
            mod(3)
            diag(0, 0)
            some_ada(len(todo))
            residual(0)
            mod(4)

            def moe(layer):
                M = lambda name: moe_sem(layer, name)
                L = 2 * layer + 1
                rms(2 + 2 * layer, sem("ss_ready"), 4 * (L + 1), D)
                normed(L)
                hT(L, L)
                diag(L, L)
                route(v, link, layer, M)
                n = v.value_load(CN[0:1, 0:1], min_val=8, max_val=MAX_ITEMS)

                def turned(wait):
                    v.wait_ge(M("tx"), wait)
                    for c in range(4, 8):
                        last = ts(XgT[:, c, :], PS[:, 1, (c - 4) * P:(c - 3) * P], MOD[:, L, 8 + c:9 + c],
                                  MOD[:, L, c:c + 1], ALU.mult, ALU.add)
                    last.then_inc(M("xgv"), 1)

                turned(1)
                v.wait_ge(*free("gate", 2 * (L + 1)))
                nc.vector.engine_nop().then_inc(M("hid"), 1)
                nc.vector.engine_nop().then_inc(M("yt"), 1)
                nc.vector.engine_nop().then_inc(M("row_out"), 16)
                with v.Fori(0, n) as i:
                    v.wait_ge(M("sil"), i + 1)
                    v.wait_ge(M("up"), i + 1)
                    tt(hid, sil, PS[:, 2, DEXP:2 * DEXP], ALU.mult).then_inc(M("hid"), 1)
                    turned(i + 2)
                    v.wait_ge(M("th"), i + 1)
                    nc.vector.tensor_copy(hidT, PS[:, 4, 0:2 * P].rearrange("p (c t) -> p c t", c=2)
                                          ).then_inc(M("hT"), 1)
                    v.wait_ge(M("down"), i + 1)
                    v.wait_ge(M("row_out"), i * 16 + 16)
                    tt(Yt[:, 0:512], PS[:, 6, :], GB[:, 0:512], ALU.mult)
                    tt(Yt[:, 512:1024], PS[:, 7, :], GB[:, 512:1024], ALU.mult).then_inc(M("yt"), 1)
                nc.vector.engine_nop().then_inc(M("yt_last"), 1)
                for b in range(NB):
                    v.wait_ge(M(f"pair_in{b}"), 32)
                    for j in range(2):
                        if b or j:
                            v.wait_ge(sem("x_done"), 8 * L + 2 * b + j)
                        stt(X[:, b, :], CB[:, 2 * b + j, :], W12[:, j, b:b + 1], X[:, b, :], ALU.mult, ALU.add
                            ).then_inc(sem("x_done"), 1)

            moe(0)

            def recurrence_masks():
                low = tmp[:, :, :].rearrange("p a b -> p (a b)").bitcast(I32)
                xr, sh = low[:, 0:P], low[:, P:2 * P]
                link(nc.vector.tensor_copy(sh, io128[:, :]))
                link(ts(xr, ones[:, :], tid[:, 0:1], None, ALU.mult))
                link(tt(xr, xr, sh, ALU.bitwise_xor))
                link(ts(LV[:, :], xr, 0.0, None, ALU.is_gt))
                for lv in range(1, LEVELS + 1):
                    link(stt(LV[:, :], xr, float(2 ** lv), LV[:, :], ALU.is_ge, ALU.add))
                link(tt(LV[:, :], LV[:, :], upper[:, :], ALU.mult))
                for k in range(4):
                    if k % 2:
                        tt(MK[:, k * P:(k + 1) * P], upper[:, :], ident[:, :], ALU.add)
                    else:
                        nc.vector.tensor_copy(MK[:, k * P:(k + 1) * P], upper[:, :])
                ts(pairs, LV[:, :], 1.0, None, ALU.is_equal)
                ts(oka[:, :], vecB[:, 72:80], -1.0, 1.0, ALU.mult, ALU.add).then_inc(sem("levels"), 1)

            def rwkv():
                rms(3, sem("ss_ready"), 12, D)
                normed(2)
                hT(2, 2)
                v.wait_ge(*free("xTa", 12))
                v.wait_ge(*free("xTv", 12))
                v.wait_ge(*full("xTa", 12))
                used = {2: ("v1", 8), 3: ("wl", 1), 4: ("al", 1), 5: ("gl", 2)}
                for m, mu in enumerate((3, 1, 4, 5, 0, 2)):
                    if m == 1:
                        recurrence_masks()
                    if m in used:
                        k, n = used[m]
                        v.wait_ge(*full(k, n))
                    for c in range(KC):
                        if m == 0:
                            tt(XX[:, c, 1:S], HT[:, c, 0:S - 1], HT[:, c, 1:S], ALU.subtract)
                            link(ts(XX[:, c, 0:1], HT[:, c, 0:1], -1.0, None, ALU.mult))
                        stt(XM[m % 2][:, c, :], XX[:, c, :], vecB[:, mu * 8 + c:mu * 8 + c + 1], HT[:, c, :],
                            ALU.mult, ALU.add).then_inc(sem("mixed"), 1)
                for c in range(KC + 1):
                    if c < KC:
                        v.wait_ge(*full("k1", c + 1))
                        nc.vector.tensor_copy(K1[:, c, :], bank("k1", c)).then_inc(drained["k1"], 1)
                        v.wait_ge(*free("k1", c + 1))
                        ts(KK[:, c, :], K1[:, c, :], vecB[:, 64 + c:65 + c], None, ALU.mult).then_inc(sem("kkr"), 1)
                    if c:
                        m = c - 1
                        if m >= 2:
                            v.wait_ge(sem("kk_unit"), m - 1)
                        v.wait_ge(*full("nrm", m + 1))
                        ts(RN[m % 2], bank("nrm", m), 1e-24, None, ALU.max).then_inc(drained["nrm"], 1)
                        v.wait_ge(*free("za", m + 1))
                        link(ts(tmp[:, 0, :], AR[:, m, :], vecB[:, 72 + m:73 + m], oka[:, m:m + 1],
                                ALU.mult, ALU.add))
                        link(tt(K1[:, m, :], K1[:, m, :], tmp[:, 0, :], ALU.mult))
                        v.wait_ge(sem("knorm"), m + 1)
                        v.wait_ge(sem("ksq"), m + 1)
                        link(nc.vector.reciprocal(RN[m % 2], RN[m % 2]))
                        tt(KK[:, m, :], KK[:, m, :], RN[m % 2], ALU.mult).then_inc(sem("kk_unit"), 1)
                v.wait_ge(sem("kk_unit"), KC)
                tt(AA[:, 0, :], AR[:, 0, :], KK[:, 0, :], ALU.mult).then_inc(sem("added_key"), 1)
                num = {k: 0 for k in ("sc", "Tn", "Tt", "R", "dS")}

                def nxt(kind):
                    num[kind] += 1
                    return num[kind] - 1

                b4 = lambda a: a.rearrange("p (j t) -> p j t", j=NB)
                for step in scan_steps():
                    kind = step[0]
                    if kind == "cumulate":
                        c = step[1]
                        if c:
                            v.wait_ge(*full("bon", c))
                        else:
                            v.wait_ge(*free("zw", KC))
                        stt(tmp[:, 0, :], R1[:, c, :], vecB[:, 80 + c:81 + c], K1[:, c, :], ALU.mult, ALU.mult
                            ).then_inc(sem("rk"), 1)
                        if c:
                            v.wait_ge(sem("prep_done"), c)
                        link(nc.vector.tensor_tensor_scan(CU, NM[:, :], SGW[:, c, :], 0.0, ALU.mult, ALU.add))
                        link(nc.vector.tensor_copy(MID[:, :], CU[:, HD - 1:S:P]))
                        tt(b4(CU), b4(CU), MID[:, :].unsqueeze(2).to_broadcast([P, NB, P]), ALU.subtract
                           ).then_inc(sem("cc"), 1)
                        v.wait_ge(sem("cc"), c + 1)
                        tt(SGW[:, c, :], CU, SGW[:, c, :], ALU.subtract).then_inc(sem("ce"), 1)
                    elif kind == "scale":
                        c = step[1]
                        v.wait_ge(sem("added_key"), c + 1)
                        v.wait_ge(sem("ee"), c + 1)
                        v.wait_ge(sem("e1"), c + 1)
                        link(tt(DD[:, c % 3, 0:NB - 1], EE[:, 0:NB - 1], EM[:, 1:NB], ALU.mult))
                        tt(R1[:, c, :], R1[:, c, :], E1, ALU.mult)
                        v.wait_ge(sem("e2"), c + 1)
                        stt(KK[:, c, :], KK[:, c, :], -1.0, SGW[:, c, :], ALU.mult, ALU.mult)
                    elif kind == "place":
                        c = step[1]
                        v.wait_ge(sem("e3"), c + 1)
                        if c == 0:
                            v.wait_ge(sem("zeroed"), 1)
                        for h in range(2):
                            lo = slice(h * HD, (h + 1) * HD)
                            last = tt(BZ[lo, h, :, :], arena[lo, 4:8:3, c * S:(c + 1) * S],
                                      CU[lo, :].unsqueeze(1).to_broadcast([HD, 2, S]), ALU.mult)
                        last.then_inc(sem("prep_done"), 1)
                    elif kind == "turn":
                        c = step[1]
                        v.wait_ge(*full("bon", c + 1))
                        nc.vector.tensor_copy(BON[:, c, :], bank("bon", c)[:, 0:8]).then_inc(drained["bon"], 1)
                        v.wait_ge(*free("bon", c + 1))
                    elif kind == "scores":
                        _, c, h, j = step
                        n = nxt("sc")
                        v.wait_ge(*full("sc", n + 1))
                        if n == 0:
                            v.wait_ge(sem("zeroed"), 3)
                        if c >= 1:
                            v.wait_ge(*full("X", 2 * LEVELS * c))
                            v.wait_ge(sem("lm_ready"), 2 * (LEVELS - 1) * c)
                        ps = bank("sc", n)
                        nc.vector.copy_predicated(LT[h][:, j, :], MK[:, 0:P], ps[:, 0:P]).then_inc(sem("lt_ready"), 1)
                        v.wait_ge(sem("unit"), 2 * c + h + 1)
                        nc.vector.copy_predicated(Tt[c % 2][h][:, j, :], pairs, ps[:, 0:P]).then_inc(sem("tt0"), 1)
                        if c >= 2:
                            v.wait_ge(*full("Y", 8 * (c - 1)))
                        nc.vector.copy_predicated(PM[c % 2][h][:, j, :, :].rearrange("p m t -> p (m t)"),
                                                  MK[:, P:4 * P], ps[:, P:4 * P]).then_inc(drained["sc"], 1)
                    elif kind == "T":
                        _, c, h, lv = step
                        n = nxt("Tt")
                        v.wait_ge(*full("Tt", n + 1))
                        if lv == 0:
                            v.wait_ge(sem("tt0"), NB * (2 * c + h + 1))
                        if lv < LEVELS - 1:
                            tt(Tt[c % 2][h], Tt[c % 2][h], b4(bank("Tt", n)), ALU.add).then_inc(drained["Tt"], 1)
                        else:
                            tt(Tt[c % 2][h][0:HD, :, HD:P], Tt[c % 2][h][0:HD, :, HD:P],
                               bank("Tt", n)[0:HD, 0:NB * HD].rearrange("p (j t) -> p j t", j=NB), ALU.add
                               ).then_inc(drained["Tt"], 1)
                    elif kind == "R":
                        _, c, h, j = step
                        n = nxt("R")
                        v.wait_ge(*full("R", n + 1))
                        if n >= 2:
                            v.wait_ge(*full("U", n - 1))
                        nc.vector.tensor_copy(RH[:, h, :], bank("R", n)[:, 0:HD]).then_inc(drained["R"], 1)
                    elif kind == "dS":
                        _, c, h, j = step
                        n = nxt("dS")
                        lo = slice(h * HD, (h + 1) * HD)
                        d = DD[lo, c % 3, j:j + 1]
                        ps = bank("dS", n)[lo, 0:HD]
                        new = ST[lo, (j + 1) % 2, :]
                        v.wait_ge(sem("prep_done"), c + 1)
                        if j == 0:
                            v.wait_ge(*full("dS", n + 1))
                            if c:
                                v.wait_ge(*full("Y", 8 * c))
                            ts(new, ps, d, None, ALU.mult).then_inc(drained["dS"], 1)
                        else:
                            v.wait_ge(*free("dS", n - 1))
                            link(ts(SD[lo, :], ST[lo, j % 2, :], d, None, ALU.mult))
                            v.wait_ge(*full("dS", n + 1))
                            stt(new, ps, d, SD[lo, :], ALU.mult, ALU.add).then_inc(drained["dS"], 1)
                    elif kind == "mean":
                        c = step[1]
                        y = SGW[:, c, :].rearrange("p (n d) -> p n d", d=HD)
                        v.wait_ge(*free("Y", 8 * (c + 1)))
                        link(red(sm[:, 0, :], y, AX, ALU.add))
                        link(ts(sm[:, 1, :], sm[:, 0, :], 1.0 / HD, None, ALU.mult))
                        tt(y, y, sm[:, 1, :].unsqueeze(2).to_broadcast([P, 8, HD]), ALU.subtract
                           ).then_inc(sem("gn_mean"), 1)
                        v3 = V1[:, :, c * P:(c + 1) * P]
                        for j in range(NB):
                            last = tt(v3[:, j, :].rearrange("p (h d) -> p h d", h=2),
                                      v3[:, j, :].rearrange("p (h d) -> p h d", h=2),
                                      BON[:, c, 2 * j:2 * j + 2].unsqueeze(2).to_broadcast([P, 2, HD]), ALU.mult)
                        last.then_inc(sem("gn_bv"), 1)
                    elif kind == "variance":
                        c = step[1]
                        v.wait_ge(sem("gn_sq"), c + 1)
                        link(red(sm[:, 0, :], KK[:, c, :].rearrange("p (n d) -> p n d", d=HD), AX, ALU.add))
                        ts(sm[:, 2, :], sm[:, 0, :], 1.0 / HD, GN_EPS, ALU.mult, ALU.add).then_inc(sem("gn_var"), 1)
                    elif kind == "output":
                        c = step[1]
                        y = SGW[:, c, :].rearrange("p (n d) -> p n d", d=HD)
                        v.wait_ge(sem("gn_rstd"), c + 1)
                        tt(y, y, sm[:, 3, :].unsqueeze(2).to_broadcast([P, 8, HD]), ALU.mult).then_inc(sem("gn_y"), 1)
                for k in range(8):
                    half, b = k // 4, k % 4
                    v.wait_ge(*full("g", k + 1))
                    if k == 0:
                        v.wait_ge(sem("y_ready"), KC)
                    cols = slice(half * 512, half * 512 + 512)
                    tt(V1[:, b, cols], V1[:, b, cols], bank("g", k), ALU.mult).then_inc(drained["g"], 1)
                v.wait_ge(*full("g", 8))
                diag(2, 2)
                residual(1)

            rwkv()
            moe(1)
            rms(5, sem("ss_ready"), 20, D)
            v.wait_ge(sem("fin_in"), 16)
            for b in range(NB):
                stt(XN[:, b, :], X[:, b, :], rstd[:, b:b + 1], LNW, ALU.mult, ALU.mult).then_inc(sem("fin"), 1)

        @block.tensor
        def _(pe):
            mm = nc.tensor.matmul

            def norm_T(n):
                for c in range(KC):
                    kind = "xTa" if c % 2 else "xTv"
                    k = 4 * n + c // 2
                    out = open_bank(pe, kind, k)
                    if c == 0:
                        pe.wait_ge(sem("xn"), NB * (n + 1))
                    for b in range(NB):
                        last = nc.tensor.transpose(out[:, b * P:(b + 1) * P], XN[:, b, c * P:(c + 1) * P], ident[:, :])
                    last.then_inc(filled[kind], 1)

            def mod(k):
                out = open_bank(pe, "mod", k)
                for j in (range(16), range(16, 24))[k] if k < 2 else range(24):
                    if j % KC == 0:
                        pe.wait_ge(sem("ada_step"), 3 * KC * max(k - 1, 0) + j + KC)
                    last = mm(out[:, j:j + 1], acc[:, j * P:(j + 1) * P], ones[:, 0:1], start=True, stop=True)
                last.then_inc(filled["mod"], 1)

            def gate(k):
                for half in range(2):
                    out = open_bank(pe, "gate", 2 * k + half)
                    pe.wait_ge(sem("diag"), 8 * k + 4 * half + 4)
                    for c in range(4):
                        last = mm(out[:, c * P:(c + 1) * P], ones[:, :], DG[:, 4 * half + c, :], start=True, stop=True)
                    last.then_inc(filled["gate"], 1)

            def rows(kind, k, b, tile, act_T, chunks_ready=None):
                out = open_bank(pe, kind, k)
                for c in range(KC):
                    if chunks_ready:
                        pe.wait_ge(chunks_ready, c + 1)
                    last = mm(out, act_T[:, c, b * P:(b + 1) * P], WR[:, tile % 2, c, :], start=(c == 0),
                              stop=(c == KC - 1))
                last.then_inc(filled[kind], 1)

            def feats(kind, k, f, tile, act_T):
                out = open_bank(pe, kind, k)
                for c in range(KC):
                    last = mm(out, WR[:, tile % 2, c, f * P:(f + 1) * P], act_T[:, c, :], start=(c == 0),
                              stop=(c == KC - 1))
                last.then_inc(filled[kind], 1)

            def hT_ready(n):
                pe.wait_ge(*free("xTv", 4 * (n + 1)))
                pe.wait_ge(*free("xTa", 4 * (n + 1)))

            def out_proj(layer, first_tile):
                for half in range(2):
                    tile_ready(pe, first_tile + half)
                    for b in range(NB):
                        rows("y", 8 * layer + 4 * half + b, b, first_tile + half, HT)

            pe.wait_ge(sem("ident_ready"), 1)
            pe.wait_ge(sem("vec_in"), 16 * 10)
            for k, r in enumerate((VA, VB)):
                out = open_bank(pe, "vec", k)
                nc.tensor.transpose(out[:, 0:104], r[0:104, :], ident[0:104, 0:104]).then_inc(filled["vec"], 1)
            pe.wait_ge(sem("ones_ready"), 1)
            norm_T(0)
            mod(0)
            pe.wait_ge(sem("h0_ready"), KC)
            for n, kind in enumerate(("q", "k")):
                tile_ready(pe, n)
                for f in range(4):
                    feats(kind, f, f, n, HT)
            mod(1)
            for n, kind in enumerate(("v", "u", "z")):
                tile_ready(pe, 2 + n)
                for b in range(NB):
                    rows(kind, b, b, 2 + n, HT)
            mod(2)
            pe.wait_ge(*free("q", 4))
            pe.wait_ge(*free("k", 4))
            pe.wait_ge(*free("v", 4))
            for n in range(NB * NHA + 3):
                if n < NB * NHA:
                    i, h = n // NHA, n % NHA
                    lo = HD * (h % 2)
                    out = open_bank(pe, "score", n)
                    if n == 0:
                        pe.wait_ge(sem("zss_ready"), 4)
                    mm(out[:, 0:(i + 1) * P], qT[lo:lo + HD, h // 2, i * P:(i + 1) * P],
                       kT[lo:lo + HD, h // 2, 0:(i + 1) * P], start=True, stop=True).then_inc(filled["score"], 1)
                if 2 <= n <= NB * NHA + 1:
                    m = n - 2
                    i = m // NHA
                    out = open_bank(pe, "pT", m)
                    pe.wait_ge(sem("pm"), m + 1)
                    for j in range(i + 1):
                        last = nc.tensor.transpose(out[:, j * P:(j + 1) * P], Pb[:, m % 3, j * P:(j + 1) * P],
                                                   ident[:, :])
                    last.then_inc(filled["pT"], 1)
                if n >= 3:
                    m = n - 3
                    i, h = m // NHA, m % NHA
                    out = open_bank(pe, "o", i) if h == 0 else bank("o", i)
                    pe.wait_ge(*free("pT", m + 1))
                    for j in range(i + 1):
                        last = mm(out[:, h * HD:(h + 1) * HD], PT[:, m % 3, j * P:(j + 1) * P],
                                  V0[:, j, h * HD:(h + 1) * HD], start=(j == 0), stop=(j == i))
                    last.then_inc(sem("pv"), 1)
                    if h == NHA - 1:
                        out = open_bank(pe, "oT", i)
                        pe.wait_ge(*free("o", i + 1))
                        for c in range(4):
                            last = nc.tensor.transpose(out[:, c * P:(c + 1) * P], OB[:, i % 2, c * P:(c + 1) * P],
                                                       ident[:, :])
                        last.then_inc(filled["oT"], 1)
            pe.wait_ge(sem("swm"), 1)
            for k in range(2):
                out = open_bank(pe, "swT", k)
                for c in range(4):
                    last = nc.tensor.transpose(out[:, c * P:(c + 1) * P], SW[:, 4 * k + c, :], ident[:, :])
                last.then_inc(filled["swT"], 1)
            for b in range(NB):
                out = open_bank(pe, "mix", b)
                pe.wait_ge(*free("swT", 2))
                pe.wait_ge(sem("zn"), b + 1)
                for g in range(NHA):
                    last = mm(out[:, g * HD:(g + 1) * HD], SWT[:, g, :], Z0[:, b, g * HD:(g + 1) * HD],
                              start=True, stop=True)
                last.then_inc(filled["mix"], 1)
            for b in range(NB):
                out = open_bank(pe, "sT", b)
                pe.wait_ge(sem("sgu_ob"), b + 1)
                for c in range(4):
                    last = nc.tensor.transpose(out[:, c * P:(c + 1) * P], OB[:, b % 2, c * P:(c + 1) * P], ident[:, :])
                last.then_inc(filled["sT"], 1)
            mod(3)
            gate(0)
            pe.wait_ge(*free("oT", 4))
            pe.wait_ge(*free("sT", 4))
            out_proj(0, 5)
            mod(4)

            def moe(layer):
                M = lambda name: moe_sem(layer, name)
                L = 2 * layer + 1
                norm_T(L)
                hT_ready(L)
                pe.wait_ge(sem("rw_in"), 16)
                out = open_bank(pe, "logit", layer)
                for b in range(NB):
                    for c in range(KC):
                        last = mm(out[:, b * NEXP:(b + 1) * NEXP], HT[:, c, b * P:(b + 1) * P], RWt[:, c, :],
                                  start=(c == 0), stop=(c == KC - 1))
                last.then_inc(filled["logit"], 1)
                out = open_bank(pe, "rank", layer)
                pe.wait_ge(M("chosen"), 1)
                pe.wait_ge(sem("moe_consts"), 5)
                mm(out[:, 0:(NB + 1) * NEXP], upper[:, :], CHX[:, :], start=True, stop=False)
                for k in range(1, NB + 1):
                    last = mm(out[:, k * NEXP:(NB + 1) * NEXP], ones[:, :], CHX[:, 0:(NB + 1 - k) * NEXP],
                              start=False, stop=(k == NB))
                last.then_inc(filled["rank"], 1)
                out = open_bank(pe, "list", layer)
                pe.wait_ge(M("hot"), 1)
                for k in range(8):
                    last = mm(out[:, 0:25], HOTR[:, k, :], HOTI[:, k, :], start=(k == 0), stop=(k == 7))
                last.then_inc(filled["list"], 1)
                gate(L)
                for kind in ("gate", "list", "rank", "logit", "xTa", "xTv"):
                    pe.wait_ge(*free(kind, {"gate": 2 * (L + 1), "list": layer + 1, "rank": layer + 1,
                                               "logit": layer + 1, "xTa": 4 * (L + 1), "xTv": 4 * (L + 1)}[kind]))
                pe.wait_ge(M("items"), 1)
                n = pe.value_load(CN[0:1, 0:1], min_val=8, max_val=MAX_ITEMS)

                def turn(wait):
                    pe.wait_ge(M("xg_in"), wait)
                    for c in range(KC):
                        last = nc.tensor.transpose(PS[:, c // 4, (c % 4) * P:(c % 4 + 1) * P],
                                                   Xg[:, c * P:(c + 1) * P], ident[:, :])
                    last.then_inc(M("tx"), 1)

                turn(16)
                with pe.Fori(0, n) as i:
                    slot = bass.ds(i % 2, 1)
                    pe.wait_ge(M("xga"), i + 1)
                    pe.wait_ge(M("xgv"), i + 1)
                    pe.wait_ge(M("w1_in"), i * 16 + 16)
                    pe.wait_ge(M("w3_in"), i * 16 + 16)
                    pe.wait_ge(M("hid"), i + 1)
                    for c in range(KC):
                        last = mm(PS[:, 2, :], XgT[:, c, :],
                                  WR[:, slot, c, :].rearrange("p s f -> p (s f)"),
                                  start=(c == 0), stop=(c == KC - 1))
                    last.then_inc(M("up"), 1)
                    turn(i * 16 + 32)
                    pe.wait_ge(M("hid"), i + 2)
                    for c in range(2):
                        last = nc.tensor.transpose(PS[:, 4, c * P:(c + 1) * P], hid[:, c * P:(c + 1) * P], ident[:, :])
                    last.then_inc(M("th"), 1)
                    pe.wait_ge(M("hT"), i + 1)
                    pe.wait_ge(M("w2_in"), i * 16 + 16)
                    pe.wait_ge(M("yt"), i + 1)
                    for half in range(2):
                        for c in range(2):
                            last = mm(PS[:, 6 + half, :], hidT[:, c, :],
                                      W2[:, slot, c, half * 512:half * 512 + 512].rearrange("p s f -> p (s f)"),
                                      start=(c == 0), stop=(c == 1))
                    last.then_inc(M("down"), 1)

            moe(0)

            def rwkv():
                pe.wait_ge(moe_sem(0, "yt_last"), 1)
                norm_T(2)
                for k in range(8):
                    if k % 4 == 0:
                        tile_ready(pe, 7 + k // 4)
                    rows("v1", k, k % 4, 7 + k // 4, XM[0], sem("mixed") if k == 0 else None)
                pe.wait_ge(sem("lora_in"), 48)

                def small(kind, k, out, w, x, m):
                    for c in range(KC):
                        if k == 0:
                            pe.wait_ge(sem("mixed"), 8 * m + c + 1)
                        last = mm(out, w[:, c, :], x[:, c, :], start=(c == 0), stop=(c == KC - 1))
                    last.then_inc(filled[kind], 1)

                small("wl", 0, open_bank(pe, "wl", 0)[0:HD, :], W1L, XM[1], 1)
                small("al", 0, open_bank(pe, "al", 0)[HD:P, :], A1L, XM[0], 2)
                small("gl", 0, open_bank(pe, "gl", 0), G1L[:, :, 0:P], XM[1], 3)
                small("gl", 1, open_bank(pe, "gl", 1)[0:32, :], G1L[:, :, P:P + 32], XM[1], 3)
                pe.wait_ge(sem("mixed"), 40)
                for k in range(8):
                    if k % 4 == 0:
                        tile_ready(pe, 9 + k // 4)
                    feats("r1", k, k % 4, 9 + k // 4, XM[0])
                pe.wait_ge(sem("mixed"), 48)
                pe.wait_ge(sem("wa2_in"), 32)
                pe.wait_ge(sem("blk_ready"), 2)
                pe.wait_ge(*free("wl", 1))
                pe.wait_ge(*free("al", 1))
                for c in range(KC + 1):
                    if c < KC:
                        if c % 4 == 0:
                            tile_ready(pe, 11 + c // 4)
                        feats("k1", c, c % 4, 11 + c // 4, XM[1])
                        mm(open_bank(pe, "zw", c), WA2[0:HD, c * P:(c + 1) * P], TWA[0:HD, :], start=True, stop=True
                           ).then_inc(filled["zw"], 1)
                        mm(open_bank(pe, "za", c), WA2[HD:P, c * P:(c + 1) * P], TWA[HD:P, :], start=True, stop=True
                           ).then_inc(filled["za"], 1)
                    if c:
                        out = open_bank(pe, "nrm", c - 1)
                        pe.wait_ge(sem("ksq"), c)
                        mm(out, blk[:, :], (CU, E1)[(c - 1) % 2], start=True, stop=True).then_inc(filled["nrm"], 1)
                num = {k: 0 for k in ("sc", "X", "Tn", "Tt", "R", "U", "Y", "dS")}

                def nxt(kind):
                    num[kind] += 1
                    return num[kind] - 1

                for step in scan_steps():
                    kind = step[0]
                    if kind == "turn":
                        c = step[1]
                        pe.wait_ge(sem("prep_done"), c + 1)
                        for h in range(2):
                            out = open_bank(pe, "bkT", 2 * c + h)
                            lo = slice(h * HD, (h + 1) * HD)
                            for q in range(2 * NB):
                                last = nc.tensor.transpose(out[:, q * HD:(q + 1) * HD],
                                                           BZ[lo, h, q % 2, q // 2 * P:(q // 2 + 1) * P],
                                                           ident[lo, lo])
                            last.then_inc(filled["bkT"], 1)
                        out = open_bank(pe, "bon", c)
                        pe.wait_ge(sem("rk"), c + 1)
                        for j in range(NB):
                            last = mm(out[:, 2 * j:2 * j + 2], tmp[:, 0, j * P:(j + 1) * P], blk[:, 0:P:HD],
                                      start=True, stop=True)
                        last.then_inc(filled["bon"], 1)
                    elif kind == "scores":
                        _, c, h, j = step
                        n = nxt("sc")
                        lo = slice(h * HD, (h + 1) * HD)
                        at = slice(c * S + j * P, c * S + (j + 1) * P)
                        out = open_bank(pe, "sc", n)
                        for m in range(2):
                            last = mm(out[:, m * 256:(m + 1) * 256].rearrange("p (a t) -> p a t", a=2),
                                      BZ[:, h, m, j * P:(j + 1) * P], arena[:, 2:7:4, at], start=True, stop=True)
                        last.then_inc(filled["sc"], 1)
                    elif kind == "lower":
                        _, c, h = step
                        out = open_bank(pe, "lo", 2 * c + h)
                        pe.wait_ge(sem("tt0"), NB * (2 * c + h + 1))
                        for j in range(NB):
                            last = nc.tensor.transpose(out[:, j * P:(j + 1) * P], Tt[c % 2][h][:, j, :], ident[:, :])
                        last.then_inc(filled["lo"], 1)
                    elif kind == "X":
                        _, c, h, lv = step
                        n = nxt("X")
                        out = open_bank(pe, "X", n)
                        if lv == 0:
                            pe.wait_ge(*free("lo", 2 * c + h + 1))
                        else:
                            pe.wait_ge(*free("Tn", 2 * (LEVELS - 1) * c + 2 * (lv - 1) + h + 1))
                        if lv < LEVELS - 1:
                            pe.wait_ge(sem("lm_ready"), 2 * (LEVELS - 1) * c + 2 * lv + h + 1)
                            for j in range(NB):
                                last = mm(out[:, j * P:(j + 1) * P], LM[h][:, j, :], Tn[h][:, j, :],
                                          start=True, stop=True)
                        else:
                            for j in range(NB):
                                last = mm(out[HD:P, j * HD:(j + 1) * HD], LT[h][0:HD, j, HD:P], Tn[h][0:HD, j, 0:HD],
                                          start=True, stop=True)
                        last.then_inc(filled["X"], 1)
                    elif kind == "T":
                        _, c, h, lv = step
                        pe.wait_ge(*free("X", 2 * LEVELS * c + 2 * lv + h + 1))
                        if lv:
                            pe.wait_ge(*free("Tt", 2 * LEVELS * c + 2 * (lv - 1) + h + 1))
                        n = nxt("Tt")
                        out = open_bank(pe, "Tt", n)
                        for j in range(NB):
                            if lv < LEVELS - 1:
                                last = mm(out[:, j * P:(j + 1) * P], XT[h][:, j, :], Tt[c % 2][h][:, j, :],
                                          start=True, stop=True)
                            else:
                                last = mm(out[0:HD, j * HD:(j + 1) * HD], XT[h][HD:P, j, 0:HD],
                                          Tt[c % 2][h][HD:P, j, HD:P], start=True, stop=True)
                        last.then_inc(filled["Tt"], 1)
                    elif kind == "N":
                        _, c, h, lv = step
                        n = nxt("Tn")
                        out = open_bank(pe, "Tn", n)
                        pe.wait_ge(*free("Tt", 2 * LEVELS * c + 2 * lv + h + 1))
                        w = P if lv < LEVELS - 2 else HD
                        for j in range(NB):
                            last = nc.tensor.transpose(out[0:w, j * w:(j + 1) * w], Tt[c % 2][h][0:w, j, 0:w],
                                                       ident[0:w, 0:w])
                        last.then_inc(filled["Tn"], 1)
                    elif kind in ("R", "U", "Y", "dS"):
                        _, c, h, j = step
                        n = nxt(kind)
                        head = slice((2 * c + h) * HD, (2 * c + h + 1) * HD)
                        lo = slice(h * HD, (h + 1) * HD)
                        V = V1[:, j, head]
                        pm = PM[c % 2][h]
                        at = slice(j * P, (j + 1) * P)
                        st = ST[lo, j % 2, :]
                        out = open_bank(pe, kind, n)
                        if kind == "R":
                            if j:
                                pe.wait_ge(*free("dS", 6 * c + 2 * (j - 1) + h + 1))
                            else:
                                pe.wait_ge(*free("sc", 8 * c + 4 * (h + 1)))
                            last = mm(out[:, 0:HD], pm[:, j, 1, :], V, start=True, stop=(j == 0))
                            if j:
                                last = mm(out[:, 0:HD], KK[lo, c, at], st, start=False, stop=True)
                            last.then_inc(filled["R"], 1)
                        elif kind == "U":
                            pe.wait_ge(*free("R", 8 * c + 2 * j + h + 1))
                            pe.wait_ge(*free("Tt", 2 * LEVELS * (c + 1)))
                            mm(out[:, 0:HD], Tt[c % 2][h][:, j, :], RH[:, h, :], start=True, stop=True
                               ).then_inc(filled["U"], 1)
                        elif kind == "Y":
                            mm(out[:, 0:HD], pm[:, j, 2, :], V, start=True, stop=False)
                            if j:
                                mm(out[:, 0:HD], R1[lo, c, at], st, start=False, stop=False)
                            pe.wait_ge(*free("U", 8 * c + 2 * j + h + 1))
                            mm(out[:, 0:HD], pm[:, j, 0, :], UU[:, h, :], start=False, stop=True
                               ).then_inc(filled["Y"], 1)
                        else:
                            pe.wait_ge(*free("bkT", 2 * (c + 1)))
                            mm(out[lo, 0:HD], BK[c % 2][:, j, 1, lo], V, start=True, stop=False)
                            mm(out[lo, 0:HD], BK[c % 2][:, j, 0, lo], UU[:, h, :], start=False, stop=True
                               ).then_inc(filled["dS"], 1)
                pe.wait_ge(sem("g2_in"), 32)
                for k in range(8):
                    half, b = k // 4, k % 4
                    out = open_bank(pe, "g", k)
                    cols = slice(half * 512, half * 512 + 512)
                    at = slice(b * P, (b + 1) * P)
                    mm(out, TG[:, 0, at], G2A[:, cols], start=True, stop=False)
                    mm(out, TG[0:32, 1, at], G2B[:, cols], start=False, stop=True).then_inc(filled["g"], 1)
                for c in range(KC):
                    out = open_bank(pe, "yT", c)
                    pe.wait_ge(*free("g", 4 * (c // 4) + 4))
                    for b in range(NB):
                        last = nc.tensor.transpose(out[:, b * P:(b + 1) * P], V1[:, b, c * P:(c + 1) * P], ident[:, :])
                    last.then_inc(filled["yT"], 1)
                gate(2)
                pe.wait_ge(*free("yT", 8))
                out_proj(1, 13)

            rwkv()
            moe(1)

    return nc


_INS = ['x', 'c', 'ada_w', 'ada_b', 'mix_w_in', 'mix_w_out', 'sgu_norm_g', 'sgu_w', 'sgu_b',
        'rwkv_mu', 'rwkv_w_rkv', 'rwkv_w_o', 'rwkv_w0', 'rwkv_w1', 'rwkv_w2', 'rwkv_a0', 'rwkv_a1', 'rwkv_a2',
        'rwkv_g1', 'rwkv_g2', 'rwkv_k_k', 'rwkv_k_a', 'rwkv_r_k', 'rwkv_ln_w', 'rwkv_ln_b',
        'router_w', 'router_b', 'moe_w1', 'moe_w3', 'moe_w2', 'final_norm_g']


def kernel(**inputs):
    import numpy as np
    import concourse.bacc as bacc
    from concourse.bass_utils import run_bass_kernel_spmd

    nc = bacc.Bacc("TRN2", target_bir_lowering=False, num_devices=1)
    arrays, io = {}, {}
    for name in _INS:
        a = np.ascontiguousarray(inputs[name])
        arrays[f"in_{name}"] = a
        io[name] = nc.dram_tensor(f"in_{name}", a.shape, mybir.dt.from_np(a.dtype), kind="ExternalInput").ap()
    io["out"] = nc.dram_tensor("out", (1, S, D), F32, kind="ExternalOutput").ap()
    build(nc, io)
    r = run_bass_kernel_spmd(nc, [arrays], core_ids=[0])
    return r.results[0]["out"]
```
